# Optimizing a Trainium2 kernel written in Bass

```python
import math
import jax, jax.numpy as jnp
from jax import lax
import numpy as np

D_MODEL = 1024
BATCH = 1
SEQ = 1024
DEPTH = 2

HEAD_DIM = 64
N_HEADS_A = 8
N_HEADS_B = 8
W_A = N_HEADS_A * HEAD_DIM
W_B = N_HEADS_B * HEAD_DIM
DILATED_PAIRS = ((128, 1), (512, 4), (2048, 16))
DSW_BLOCK = 64
GRID_W = 64
NA_ROWS = 8
NA_COLS = 16
NA_COL_BLOCK = 16
NA_COL_REGION = NA_COL_BLOCK + NA_COLS
N_HEADS_C = D_MODEL // (2 * HEAD_DIM)
DIFF_BLOCK = 128
D_FF = -(-8 * D_MODEL // (3 * 256)) * 256
RMS_EPS = 1e-6
SUBLN_EPS = 1e-5

kernel_name = "hybrid_dilated_natten_diffattn_encoder"

def rmsnorm(x, g, eps=RMS_EPS):
    xf = x.astype(jnp.float32)
    y = xf * lax.rsqrt(jnp.mean(xf * xf, axis=-1, keepdims=True) + eps)
    return (y * g.astype(jnp.float32)).astype(x.dtype)

def alibi_slopes(n):
    return jnp.exp2(-8.0 * jnp.arange(1, n + 1, dtype=jnp.float32) / n)

def lambda_init_fn(layer):
    return 0.8 - 0.6 * math.exp(-0.3 * layer)

def swiglu(h, w_gate, w_up, w_down):
    return (jax.nn.silu(h @ w_gate) * (h @ w_up)) @ w_down

def dilated_window_branch(q, k, v, slopes, window, dilation):
    B, H, T, Dh = q.shape
    half = window // (2 * dilation)
    L = T // dilation
    nb = -(-L // DSW_BLOCK)
    Lq = nb * DSW_BLOCK
    K = DSW_BLOCK + 2 * half

    def strided(a):
        return a.reshape(B, H, L, dilation, Dh).transpose(0, 1, 3, 2, 4)

    qs = jnp.pad(strided(q), ((0, 0), (0, 0), (0, 0), (0, Lq - L), (0, 0)))
    kpad = ((0, 0), (0, 0), (0, 0), (half, Lq - L + half), (0, 0))
    ks = jnp.pad(strided(k), kpad)
    vs = jnp.pad(strided(v), kpad)
    key_idx = np.arange(nb)[:, None] * DSW_BLOCK + np.arange(K)[None, :]
    kb = ks[:, :, :, key_idx, :]
    vb = vs[:, :, :, key_idx, :]
    qb = qs.reshape(B, H, dilation, nb, DSW_BLOCK, Dh)
    off = np.arange(K)[None, :] - half - np.arange(DSW_BLOCK)[:, None]
    key_j = key_idx - half
    valid = ((np.abs(off)[None] <= half)
             & (key_j[:, None, :] >= 0) & (key_j[:, None, :] < L))
    s = jnp.einsum('bhrnqd,bhrnkd->bhrnqk', qb, kb) * (HEAD_DIM ** -0.5)
    dist = (np.abs(off) * dilation).astype(np.float32)
    s = s - (slopes[:, None, None] * dist[None])[None, :, None, None]
    s = jnp.where(valid[None, None, None], s, -jnp.inf)
    m = jnp.max(s, axis=-1, keepdims=True)
    p = jnp.exp(s - m)
    l = jnp.sum(p, axis=-1, keepdims=True)
    o = jnp.einsum('bhrnqk,bhrnkd->bhrnqd', p, vb) / l
    lse = (m + jnp.log(l))[..., 0]
    o = o.reshape(B, H, dilation, Lq, Dh)[:, :, :, :L].transpose(0, 1, 3, 2, 4).reshape(B, H, T, Dh)
    lse = lse.reshape(B, H, dilation, Lq)[..., :L].transpose(0, 1, 3, 2).reshape(B, H, T)
    return o, lse

def dilated_mixture_attention(q, k, v):
    H = q.shape[1]
    slopes = alibi_slopes(H)
    outs, lses = [], []
    for window, dilation in DILATED_PAIRS:
        o, lse = dilated_window_branch(q, k, v, slopes, window, dilation)
        outs.append(o)
        lses.append(lse)
    wts = jax.nn.softmax(jnp.stack(lses, axis=0), axis=0)
    y = wts[0][..., None] * outs[0]
    for i in range(1, len(outs)):
        y = y + wts[i][..., None] * outs[i]
    return y

def neighborhood_attention(q, k, v, rpb):
    B, H, T, Dh = q.shape
    rows = T // GRID_W
    kh = min(NA_ROWS, rows)
    n_cb = GRID_W // NA_COL_BLOCK
    qg = q.reshape(B, H, rows, GRID_W, Dh)
    kg = k.reshape(B, H, rows, GRID_W, Dh)
    vg = v.reshape(B, H, rows, GRID_W, Dh)
    cb_start = np.clip(np.arange(n_cb) * NA_COL_BLOCK - NA_COLS // 2, 0, GRID_W - NA_COL_REGION)
    key_cols = cb_start[:, None] + np.arange(NA_COL_REGION)[None, :]
    q_cols = np.arange(GRID_W).reshape(n_cb, NA_COL_BLOCK)
    wc = np.clip(q_cols - NA_COLS // 2, 0, GRID_W - NA_COLS)[..., None]
    kc = key_cols[:, None, :]
    col_valid = (kc >= wc) & (kc < wc + NA_COLS)
    col_bias_idx = np.clip(kc - q_cols[..., None] + NA_COLS - 1, 0, 2 * NA_COLS - 2)
    scale = HEAD_DIM ** -0.5

    def row_step(r):
        rs = jnp.clip(r - kh // 2, 0, rows - kh)
        k_rows = lax.dynamic_slice_in_dim(kg, rs, kh, axis=2)
        v_rows = lax.dynamic_slice_in_dim(vg, rs, kh, axis=2)
        q_row = lax.dynamic_index_in_dim(qg, r, axis=2, keepdims=False)
        k_blk = k_rows[:, :, :, key_cols, :]
        v_blk = v_rows[:, :, :, key_cols, :]
        q_blk = q_row.reshape(B, H, n_cb, NA_COL_BLOCK, Dh)
        s = jnp.einsum('bhcqd,bhrckd->bhcqrk', q_blk, k_blk) * scale
        row_idx = (rs + jnp.arange(kh) - r + NA_ROWS - 1)[None, None, :, None]
        bias = rpb[:, row_idx, col_bias_idx[:, :, None, :]]
        s = s + bias[None].astype(jnp.float32)
        s = jnp.where(col_valid[:, :, None, :], s, -jnp.inf)
        p = jax.nn.softmax(s.reshape(B, H, n_cb, NA_COL_BLOCK, kh * NA_COL_REGION), axis=-1)
        p = p.reshape(s.shape)
        o = jnp.einsum('bhcqrk,bhrckd->bhcqd', p, v_blk)
        return o.reshape(B, H, GRID_W, Dh)

    out = lax.map(row_step, jnp.arange(rows))
    return out.transpose(1, 2, 0, 3, 4).reshape(B, H, T, Dh)

def differential_attention(q, k, v, lam):
    B, H, _, T, Dh = q.shape
    slopes = alibi_slopes(H)
    nq = T // DIFF_BLOCK
    q_blocks = q.reshape(B, H, 2, nq, DIFF_BLOCK, Dh).transpose(3, 0, 1, 2, 4, 5)
    kpos = jnp.arange(T)
    scale = Dh ** -0.5

    def block(args):
        qb, start = args
        s = jnp.einsum('bhiqd,bhikd->bhiqk', qb, k) * scale
        qpos = start + jnp.arange(DIFF_BLOCK)
        dist = jnp.abs(qpos[:, None] - kpos[None, :]).astype(jnp.float32)
        s = s - (slopes[:, None, None] * dist[None])[None, :, None]
        p = jax.nn.softmax(s, axis=-1)
        a = p[:, :, 0] - lam * p[:, :, 1]
        return jnp.einsum('bhqk,bhkd->bhqd', a, v)

    out = lax.map(block, (q_blocks, jnp.arange(nq) * DIFF_BLOCK))
    return out.transpose(1, 2, 0, 3, 4).reshape(B, H, T, 2 * Dh)

def even_mixer(h, w_in, w_out, rpb):
    B, T, _ = h.shape
    proj = (h @ w_in).astype(jnp.float32)
    cuts = np.cumsum([W_A, W_A, W_A, W_B, W_B])
    qa, ka, va, qb, kb, vb = jnp.split(proj, cuts, axis=-1)

    def heads(a):
        return a.reshape(B, T, -1, HEAD_DIM).transpose(0, 2, 1, 3)

    ya = dilated_mixture_attention(heads(qa), heads(ka), heads(va))
    yb = neighborhood_attention(heads(qb), heads(kb), heads(vb), rpb)
    y = jnp.concatenate([ya, yb], axis=1).transpose(0, 2, 1, 3).reshape(B, T, W_A + W_B)
    return y.astype(h.dtype) @ w_out

def odd_mixer(h, w_qkv, w_out, lam_q1, lam_k1, lam_q2, lam_k2, subln, layer):
    B, T, _ = h.shape
    proj = (h @ w_qkv).astype(jnp.float32)
    q, k, v = jnp.split(proj, 3, axis=-1)
    q = q.reshape(B, T, N_HEADS_C, 2, HEAD_DIM).transpose(0, 2, 3, 1, 4)
    k = k.reshape(B, T, N_HEADS_C, 2, HEAD_DIM).transpose(0, 2, 3, 1, 4)
    v = v.reshape(B, T, N_HEADS_C, 2 * HEAD_DIM).transpose(0, 2, 1, 3)
    lam_init = lambda_init_fn(layer)
    f32 = jnp.float32
    lam = (jnp.exp(jnp.sum(lam_q1.astype(f32) * lam_k1.astype(f32)))
           - jnp.exp(jnp.sum(lam_q2.astype(f32) * lam_k2.astype(f32))) + lam_init)
    y = differential_attention(q, k, v, lam)
    y = rmsnorm(y, subln, SUBLN_EPS) * (1.0 - lam_init)
    y = y.transpose(0, 2, 1, 3).reshape(B, T, N_HEADS_C * 2 * HEAD_DIM)
    return y.astype(h.dtype) @ w_out

def setup_inputs(seed: int = 0) -> dict:
    key = jax.random.key(seed)
    ks = jax.random.split(key, 24)
    f32 = jnp.float32

    def w(k, shape, fan_in):
        return jax.random.normal(k, shape, f32) * fan_in ** -0.5

    def gain(k, n):
        return 1.0 + 0.02 * jax.random.normal(k, (n,), f32)

    D = D_MODEL
    WC = N_HEADS_C * 2 * HEAD_DIM
    return {
        "x": jax.random.normal(ks[0], (BATCH, SEQ, D), f32),
        "a0_norm": gain(ks[1], D),
        "a0_w_in": w(ks[2], (D, 3 * W_A + 3 * W_B), D),
        "a0_w_out": w(ks[3], (W_A + W_B, D), W_A + W_B),
        "a0_rpb": 0.1 * jax.random.normal(ks[4], (N_HEADS_B, 2 * NA_ROWS - 1, 2 * NA_COLS - 1), f32),
        "f0_norm": gain(ks[5], D),
        "f0_w_gate": w(ks[6], (D, D_FF), D),
        "f0_w_up": w(ks[7], (D, D_FF), D),
        "f0_w_down": w(ks[8], (D_FF, D), D_FF),
        "a1_norm": gain(ks[9], D),
        "a1_w_qkv": w(ks[10], (D, 3 * WC), D),
        "a1_w_out": w(ks[11], (WC, D), WC),
        "a1_lam_q1": 0.1 * jax.random.normal(ks[12], (HEAD_DIM,), f32),
        "a1_lam_k1": 0.1 * jax.random.normal(ks[13], (HEAD_DIM,), f32),
        "a1_lam_q2": 0.1 * jax.random.normal(ks[14], (HEAD_DIM,), f32),
        "a1_lam_k2": 0.1 * jax.random.normal(ks[15], (HEAD_DIM,), f32),
        "a1_subln": gain(ks[16], 2 * HEAD_DIM),
        "f1_norm": gain(ks[17], D),
        "f1_w_gate": w(ks[18], (D, D_FF), D),
        "f1_w_up": w(ks[19], (D, D_FF), D),
        "f1_w_down": w(ks[20], (D_FF, D), D_FF),
        "final_norm": gain(ks[21], D),
    }

def reference(x, a0_norm, a0_w_in, a0_w_out, a0_rpb, f0_norm, f0_w_gate, f0_w_up, f0_w_down,
              a1_norm, a1_w_qkv, a1_w_out, a1_lam_q1, a1_lam_k1, a1_lam_q2, a1_lam_k2, a1_subln,
              f1_norm, f1_w_gate, f1_w_up, f1_w_down, final_norm):
    ffn_params = [(f0_norm, f0_w_gate, f0_w_up, f0_w_down),
                  (f1_norm, f1_w_gate, f1_w_up, f1_w_down)]
    for layer in range(DEPTH):
        if layer % 2 == 0:
            x = x + even_mixer(rmsnorm(x, a0_norm), a0_w_in, a0_w_out, a0_rpb)
        else:
            x = x + odd_mixer(rmsnorm(x, a1_norm), a1_w_qkv, a1_w_out,
                              a1_lam_q1, a1_lam_k1, a1_lam_q2, a1_lam_k2, a1_subln, layer)
        g, wg, wu, wd = ffn_params[layer]
        x = x + swiglu(rmsnorm(x, g), wg, wu, wd)
    return rmsnorm(x, final_norm)


_drawn_inputs = setup_inputs


def setup_inputs(seed=0):
    import zlib

    import numpy as np

    out = dict(_drawn_inputs(seed))
    spreads = {}
    factors = {'a0_norm': 5.161,
     'a0_rpb': 4.173,
     'f0_norm': 2.894,
     'a1_norm': 3.099,
     'a1_lam_q2': 200.0,
     'a1_subln': 26.054,
     'f1_norm': 14.59,
     'final_norm': 20.719}
    for name, (base, spread) in spreads.items():
        noise = np.random.default_rng([zlib.crc32(name.encode()), seed]).standard_normal(out[name].shape)
        drawn = base * np.exp(spread * noise) if base else spread * noise
        out[name] = __import__('jax').numpy.asarray(drawn.astype(out[name].dtype))
    for name, factor in factors.items():
        out[name] = (out[name] * factor).astype(out[name].dtype)
    return out
```

```python
import math

import numpy as np
import concourse.bass as bass
from concourse import mybir

D = 1024
T = 1024
KC = D // 128
DH = 64
F = 2816
FT = F // 128
NP = 8
NQ = T // 128
RMS_EPS = 1e-6
SUBLN_EPS = 1e-5
LAM_INIT = 0.8 - 0.6 * math.exp(-0.3)
GRID, ROWS, COLS = 64, 8, 16
BIG = 1e30
BIAS_W = T + (NQ - 1) * 128
EDGE_ROWS, MID_ROWS = 14, 10
TAB_B = (EDGE_ROWS + MID_ROWS) * GRID

PROJ = 3 * NP
W_ATTN = [0, PROJ + KC + 2 * FT]
W_OUT = [w + PROJ for w in W_ATTN]
W_FFN = [w + KC for w in W_OUT]
N_STRIPS = 2 * (PROJ + KC + 2 * FT)


def key_tiles(kind, n):
    if kind != "B":
        return 0, NQ
    lo = max(0, min(2 * n - ROWS // 2, 2 * NQ - ROWS))
    hi = max(0, min(2 * n + 1 - ROWS // 2, 2 * NQ - ROWS)) + ROWS
    return lo // 2, (hi + 1) // 2 - lo // 2


def bias_start(kind, n):
    if kind != "B":
        return 128 * (NQ - 1 - n)
    first = 2 * key_tiles("B", n)[0] - 2 * n
    if key_tiles("B", n)[1] == 5:
        return (EDGE_ROWS + first + 4) * GRID
    return (first + 6) * GRID


def build(nc, x_in, wstrips, wdown, gains, subln, lams, ali_a, ali_c, tab_b, out):
    f32, f32r = mybir.dt.float32, mybir.dt.float32r
    ALU, ACT = mybir.AluOpType, mybir.ActivationFunctionType

    place = [-(-nc.sbuf_base // 64) * 64]

    def sb(name, shape, dt=f32):
        size = int(np.prod(shape[1:])) * 4
        t = nc.alloc_sbuf_tensor_at(name, shape, dt, offset=place[0])
        place[0] += -(-size // 32) * 32
        return t

    HH = sb("HH", [128, KC, T], f32r)
    HL = sb("HL", [128, KC, T], f32r)
    RSTD = sb("RSTD", [128, T])
    WS = sb("WS", [128, 2, 2, 1024], f32r)
    WR = sb("WR", [128, 2, 512])
    IDENT = sb("IDENT", [128, 128])
    ONES = sb("ONES", [128, 128])
    GAIN = sb("GAIN", [128, 5, KC])
    SUBG = sb("SUBG", [128, 2])
    NEGLAM = sb("NEGLAM", [128, 4])
    EPS = sb("EPS", [128, 2])
    ST = sb("ST", [128, 2, 8])
    region = place[0]

    XY = sb("XY", [128, 4, 128], f32r)
    KS = sb("KS", [128, 2, 2, T], f32r)
    QR = sb("QR", [128, 2, T])
    VS = sb("VS", [128, 2, NQ, 256], f32r)
    BIAS = sb("BIAS", [128, 2, 2, BIAS_W])
    AT = sb("AT", [128, 2, NQ, 2, 256], f32r)
    E0 = sb("E0", [128, T])
    E1 = sb("E1", [128, 2, T])
    YS = sb("YS", [128, 2, 256])
    assert place[0] <= nc.sbuf_usable_end
    place[0] = region
    X = sb("X", [128, KC, T])
    SQ = sb("SQ", [128, 2, T])
    ACC = sb("ACC", [128, T])
    shared = place[0]
    LV = sb("LV", [128, 4, DH])
    LP = sb("LP", [128, 2, DH])
    place[0] = shared
    YL = sb("YL", [128, 2, T])
    YH = sb("YH", [128, KC, T], f32r)
    YO = sb("YO", [128, KC, T], f32r)
    assert place[0] <= nc.sbuf_usable_end
    place[0] = shared
    DR = sb("DR", [128, 1024])
    DS = sb("DS", [128, 2, 1024], f32r)
    SIL = sb("SIL", [128, T])
    UT = sb("UT", [128, T])
    PROD = sb("PROD", [128, T])
    AH = sb("AH", [128, T], f32r)
    AL = sb("AL", [128, T], f32r)

    y_dram = nc.dram_tensor("y_scratch", [KC, 128, T], f32, kind="Internal").ap()
    x_dram = nc.dram_tensor("x_scratch", [128, KC, T], f32, kind="Internal").ap()

    PS = nc.alloc_psum_tensor("PS", [128, 8, 512], f32)
    S_BANK, T_BANK, PV_BANK, FILL_BANK = (0, 2), 4, 6, 7
    G_BANK, U_BANK, D_BANK, SSQ_BANK = 0, 2, 4, 4

    def banks(a, n, w=512):
        return PS[:, a:a + n, 0:w].rearrange("p a b -> p (a b)")

    def f(ap):
        return ap.bitcast(f32)

    S = {}
    for name in ("ones_ready ident_ready gains_full consts_ready lam_ready acc_zero "
                 "raw_full0 raw_full1 w_hi w_lo "
                 "x_full0 x_full1 x_full2 x_full3 x_saved "
                 "sq_done xhi_done xlo_done sadd ssq_done sqrt_done rstd_done "
                 "fill_done fill_evac kmul_done khi_done tv_done vhi_done vlo_done "
                 "xy_act xy_dve bias_full0 bias_full1 bneg_done qk_done ttr_done exp_done rec_done "
                 "p0_ready p1_ready c1_ready escaled t_done hi_done lo_done pv_done y_copy y_done "
                 "y_out0 y_out1 yl_full0 yl_full1 yhi_done ylo_done ysq_done yssq_done ysqrt_done yrec_done ynorm_done "
                 "dve_passed pool_passed op_done op_free g_done u_done gmul_done sil_done umul_done prod_done ahi_done alo_done "
                 "d_full d_hi d_lo d_done d_free xy_zero out_ready out_full").split():
        S[name] = nc.alloc_semaphore(name)

    def unit(P, n, m, kind):
        return 8 * P + 2 * (n // 2) + m if kind != "C" else 64 + 4 * (P - 8) + n // 2

    def t_count(P, n, m, kind):
        return 16 * P + 2 * n + m + 1 if kind != "C" else 128 + 8 * (P - 8) + n + 1

    def iterations(eng, body, head, layer):
        if layer == 0:
            with eng.Fori(0, 2) as i:
                head(2 * i, 0, "A")
                body(2 * i, 0, "A", "A", True)
                body(2 * i + 1, 1, "A", "AB", False)
            head(4, 0, "B")
            for P in range(4, 8):
                body(P, P % 2, "B", "B" if P < 7 else None, P < 7)
        else:
            head(8, 0, "C")
            with eng.Fori(0, 3) as i:
                for par in range(2):
                    body(8 + 2 * i + par, par, "C", "C", True)
            body(14, 0, "C", "C", True)
            body(15, 1, "C", None, False)

    FILLS = [(0, 0, 24), (1, 0, 24), (2, 0, 24), (3, 0, 12), (3, 12, 24), (4, 0, 24), (5, 0, 12), (5, 12, 24)]
    EVAC_AT = {1: 0, 2: 1, 3: 2, 5: 3, 6: 4}
    TV_AT = {2: 0, 4: 1}
    SPLIT_AT = {0: 4, 3: 5, 6: 6}

    def w_base(P):
        return 3 * P if not isinstance(P, int) or P < 8 else W_ATTN[1] + 3 * (P - 8)

    def strip_of(P, layer):
        return 3 * P if layer == 0 else 3 * P + (W_ATTN[1] - 24)

    def sync_program(e):
        def raw(w):
            for x in range(2):
                if not (isinstance(w, int) and w == 0):
                    e.wait_ge(S["w_lo"], 2 * w + x - 1)
                e.dma_start(WR[:, x, :], wstrips[w, x]).then_inc(S[f"raw_full{x}"], 16)

        def load_x(src):
            for c in range(4):
                e.dma_start(X[:, 2 * c:2 * c + 2, :], src[:, 2 * c:2 * c + 2, :]).then_inc(S[f"x_full{c}"], 16)

        def bias(P, par, kind):
            e.wait_ge(S["ttr_done"], 1 + 16 * (P - 1) if not isinstance(P, int) or P else 1)
            if kind == "C":
                e.dma_start(BIAS[:, par, 0, :], ali_c[P - 8]).then_inc(S[f"bias_full{par}"], 16)
            else:
                src, w = (ali_a, BIAS_W) if kind == "A" else (tab_b, TAB_B)
                pair = P if kind == "A" else P - 4
                e.dma_start(BIAS[:, par, :, 0:w], src[pair]).then_inc(S[f"bias_full{par}"], 16)

        def attention(layer):
            P0 = 8 * layer
            kind = "AC"[layer]
            w0 = strip_of(P0, layer)
            raw(w0 + 2)
            e.wait_ge(S["rstd_done"], 2 * layer + 1)
            bias(P0, 0, kind)
            raw(w0 + 3)
            raw(w0 + 4)

            def body(P, par, kind, nxt, looks):
                if nxt is None:
                    return
                w = strip_of(P, layer)
                raw(w + 5)
                if nxt != "AB":
                    bias(P + 1, 1 - par, nxt)
                raw(w + 6)
                raw(w + 7)

            if layer == 0:
                with e.Fori(0, 2) as i:
                    for par in range(2):
                        P = 2 * i + par
                        w = strip_of(P, layer)
                        raw(w + 5)
                        e.wait_ge(S["ttr_done"], 1 + 16 * P)
                        e.dma_start(BIAS[:, 1 - par, :, :], ali_a[P + 1]).then_inc(S[f"bias_full{1 - par}"], 16)
                        raw(w + 6)
                        raw(w + 7)
                for P in range(4, 8):
                    body(P, P % 2, "B", "B" if P < 7 else None, True)
            else:
                iterations(e, body, lambda *a: None, 1)

        def out_projection(o):
            last = 8 * o + 7
            kind = "BC"[o]
            e.wait_ge(S["y_out0"], 1 + 16 * (32 if o == 0 else 48))
            e.wait_ge(S["y_out1"], 1 + 16 * (32 if o == 0 else 48))
            for k in range(KC):
                if k >= 2:
                    e.wait_ge(S["ylo_done"], 8 * o + k - 1)
                e.dma_start(YL[:, k % 2, :], y_dram[k]).then_inc(S[f"yl_full{k % 2}"], 16)
                if k == 1:
                    load_x(x_in if o == 0 else x_dram)
            with e.Fori(0, KC // 2) as i:
                for b in range(2):
                    raw(W_OUT[o] + 2 * i + b + 2)

        def ffn(n):
            e.wait_ge(S["op_done"], 1 + 16 * (n + 1))

            def body(t, last=False):
                w = W_FFN[n] + 2 * t
                e.wait_ge(S["d_lo"], 1 + FT * n + t)
                e.dma_start(DR[:, :], wdown[FT * n + t]).then_inc(S["d_full"], 16)
                if not last:
                    raw(w + 2)
                    raw(w + 3)

            with e.Fori(0, FT - 1) as t:
                body(t)
            body(FT - 1, last=n == 1)

        e.dma_start(GAIN[:, :, :], gains).then_inc(S["gains_full"], 16)
        e.dma_start(LV[:, :, :], lams.partition_broadcast(128)).then_inc(S["gains_full"], 16)
        e.dma_start(SUBG[:, 0:1], subln).then_inc(S["gains_full"], 16)
        for c in range(2):
            e.dma_start(X[:, 2 * c:2 * c + 2, :], x_in[:, 2 * c:2 * c + 2, :]).then_inc(S[f"x_full{c}"], 16)
        for x in range(2):
            e.dma_start(WR[:, x, :], wstrips[0, x]).then_inc(S[f"raw_full{x}"], 16)
        for c in range(2, 4):
            e.dma_start(X[:, 2 * c:2 * c + 2, :], x_in[:, 2 * c:2 * c + 2, :]).then_inc(S[f"x_full{c}"], 16)
        raw(1)
        attention(0)
        out_projection(0)
        ffn(0)
        e.wait_ge(S["d_free"], 4 + 16 * FT)
        e.dma_start(x_dram, X[:, :, :]).then_inc(S["x_saved"], 16)
        e.wait_ge(S["x_saved"], 16)
        attention(1)
        out_projection(1)
        ffn(1)
        for k in range(KC):
            e.wait_ge(S["out_ready"], k + 1)
            e.dma_start(out[:, k, :], X[:, k, :]).then_inc(S["out_full"], 16)
        e.wait_ge(S["out_full"], 16 * KC)

    def pool_program(e):
        e.memset(ONES[:, :], 1.0).then_inc(S["ones_ready"], 1)
        e.memset(IDENT[:, :], 0.0).then_inc(S["ident_ready"], 1)
        e.memset(EPS[:, 0:1], RMS_EPS).then_inc(S["ones_ready"], 1)
        e.memset(EPS[:, 1:2], SUBLN_EPS).then_inc(S["ones_ready"], 1)
        e.wait_ge(S["ident_ready"], 1)
        e.affine_select(out=IDENT[:, :], in_=IDENT[:, :], compare_op=ALU.not_equal, fill=1.0, base=0,
                        pattern=[[-1, 128]], channel_multiplier=1).then_inc(S["ident_ready"], 1)

        def norm1(P, n, kind):
            k0, nk = key_tiles(kind, n)
            e.wait_ge(S["rec_done"], 16 * P + 2 * n + 2)
            e.sem_inc(S["pool_passed"], 1)
            e.tensor_scalar(E1[:, n % 2, 0:128 * nk], E1[:, n % 2, 0:128 * nk], ST[:, n % 2, 5:6], None,
                            ALU.mult).then_inc(S["p1_ready"], 1)

        def head(P, par, kind):
            norm1(P, 0, kind)

        def body(P, par, kind, nxt, looks):
            for n in range(NQ):
                if n < NQ - 1:
                    norm1(P, n + 1, kind)
                elif looks:
                    norm1(P + 1, 0, kind)

        iterations(e, body, head, 0)

    def act_program(e):
        def w_split(w, slot, used=None):
            if used:
                e.wait_ge(S[used[0]], used[1])
            for x in range(2):
                e.wait_ge(S[f"raw_full{x}"], 16 * w + 16)
                e.activation(WS[:, slot, 0, 512 * x:512 * x + 512], WR[:, x, :], ACT.Copy).then_inc(S["w_hi"], 1)

        def prep_chunk(N, j, b):
            if not (isinstance(j, int) and 8 * N + j < 1):
                e.wait_ge(S["sadd"], 8 * N + j - 1)
            e.activation(SQ[:, b, :], X[:, j, :], ACT.Square).then_inc(S["sq_done"], 1)
            if N < 4:
                e.activation(HH[:, j, :], X[:, j, :], ACT.Copy, scale=GAIN[:, N, bass.ds(j, 1)]).then_inc(S["xhi_done"], 1)

        def root(N):
            e.wait_ge(S["ssq_done"], N + 1)
            e.activation(RSTD[:, :], banks(SSQ_BANK, 2), ACT.Sqrt, scale=1.0 / D, bias=EPS[:, 0:1]).then_inc(S["sqrt_done"], 1)

        def xy(P, par, n):
            e.wait_ge(S["fill_evac"], 6 * P + (5 if n < 4 else 6))
            e.wait_ge(S["qk_done"], 1 + 16 * P + 2 * n)
            q = QR[:, par, 128 * n:128 * n + 128]
            e.activation(XY[0:64, 0, :], q[0:64], ACT.Copy).then_inc(S["xy_act"], 1)
            e.activation(XY[64:128, 1, :], q[64:128], ACT.Copy).then_inc(S["xy_act"], 1)

        def exp(P, n, m, kind):
            k0, nk = key_tiles(kind, n)
            e.wait_ge(S["ttr_done"], 1 + 16 * P + 2 * n + m + 1)
            t = (E0[:, 0:128 * nk] if m == 0 else E1[:, n % 2, 0:128 * nk])
            e.activation(t, t, ACT.Exp, scale=-1.0, bias=ST[:, n % 2, m:m + 1],
                         accum_out=ST[:, n % 2, 2 + m:3 + m]).then_inc(S["exp_done"], 1)

        def escale(P, n):
            e.wait_ge(S["c1_ready"], 8 * P + n + 1 - 64)
            e.activation(E1[:, n % 2, :], E1[:, n % 2, :], ACT.Copy, scale=ST[:, n % 2, 6:7]).then_inc(S["escaled"], 1)

        def khi(P, par, kk):
            e.wait_ge(S["kmul_done"], 2 * P + kk + 1)
            c = 512 * kk
            e.activation(KS[0:64, par, 0, c:c + 512], PS[0:64, FILL_BANK, :], ACT.Copy).then_inc(S["khi_done"], 1)
            e.activation(KS[64:128, par, 1, c:c + 512], PS[64:128, FILL_BANK, :], ACT.Copy).then_inc(S["khi_done"], 1)

        def vhi(P, par, vv, kind):
            e.wait_ge(S["tv_done"], 2 * P + vv + 1)
            if kind == "C":
                dst = VS[:, par, 4 * vv:4 * vv + 4, 0:128]
                src = PS[:, PV_BANK, :].rearrange("p (k d) -> p k d", k=4)
            else:
                dst = VS[:, par, 4 * vv:4 * vv + 4, :].rearrange("p k (m s d) -> p k m s d", m=2, s=2)[:, :, :, 0, :]
                src = PS[:, PV_BANK, :].rearrange("p (k m d) -> p k m d", k=4, m=2)
            e.activation(dst, src, ACT.Copy).then_inc(S["vhi_done"], 1)

        def hi(P, n, m, kind):
            k0, nk = key_tiles(kind, n)
            b = m if kind != "C" else (n // 2) % 2
            e.wait_ge(S["t_done"], t_count(P, n, m, kind))
            e.wait_ge(S["pv_done"], unit(P, n, m, kind) + 1)
            c = 128 * (n % 2)
            e.activation(AT[:, b, k0:k0 + nk, 0, c:c + 128],
                         banks(T_BANK, 2)[:, 0:128 * nk].rearrange("p (k q) -> p k q", k=nk),
                         ACT.Copy).then_inc(S["hi_done"], 1)

        def y_copy(P, n, m, kind):
            u = unit(P, n, m, kind)
            e.wait_ge(S["pv_done"], u + 3)
            e.wait_ge(S[f"y_out{m}"], 1 + 64 * P + 16 * (n // 2))
            e.activation(YS[0:64, m, :], PS[64:128, PV_BANK, 0:256], ACT.Copy).then_inc(S["y_copy"], 1)

        def y_dma(P, n, m, kind):
            e.wait_ge(S["y_done"], 1 + unit(P, n, m, kind) + 1)
            c = 256 * (n // 2)
            if kind == "C":
                b = (n // 2) % 2
                e.dma_start(y_dram[P - 8, :, c:c + 256], YS[:, b, :]).then_inc(S[f"y_out{b}"], 16)
            else:
                e.dma_start(y_dram[P, 64 * m:64 * m + 64, c:c + 256], YS[0:64, m, :]).then_inc(S[f"y_out{m}"], 16)

        def attention(layer):
            P0, kind = 8 * layer, "AC"[layer]
            w0 = strip_of(P0, layer)
            w_split(w0 + 1, 1, ("u_done", FT * layer) if layer else None)
            w_split(w0 + 2, 0, ("fill_done", 6 * P0 + 2))
            vhi(P0, 0, 0, kind)
            khi(P0, 0, 0)
            vhi(P0, 0, 1, kind)
            khi(P0, 0, 1)
            w_split(w0 + 3, 1, ("fill_done", 6 * P0 + 4))

            def start(P, par, kind):
                xy(P, par, 0)
                exp(P, 0, 0, kind)
                xy(P, par, 1)
                exp(P, 0, 1, kind)
                if kind == "C":
                    escale(P, 0)

            def body(P, par, kind, nxt, looks):
                w = strip_of(P, layer)
                for n in range(NQ):
                    after = n + 1 if n < NQ - 1 else 8
                    go = n < NQ - 1 or looks
                    Pn, nn, parn = (P, n + 1, par) if n < NQ - 1 else (P + 1, 0, 1 - par)
                    if nxt and EVAC_AT.get(n) in (2, 3):
                        khi(P + 1, 1 - par, EVAC_AT[n] - 2)
                    hi(P, n, 0, kind)
                    if go:
                        exp(Pn, nn, 0, kind)
                    if n < NQ - 2:
                        xy(P, par, n + 2)
                    elif looks:
                        xy(P + 1, 1 - par, n - 6)
                    if kind != "C":
                        hi(P, n, 1, kind)
                    if go:
                        exp(Pn, nn, 1, kind)
                        if kind == "C":
                            escale(Pn, nn)
                    if nxt and n in TV_AT:
                        vhi(P + 1, 1 - par, TV_AT[n], kind)
                    if n % 2 and kind != "C":
                        y_copy(P, n, 0, kind)
                    if nxt and n in SPLIT_AT:
                        w_split(w + SPLIT_AT[n], (par + SPLIT_AT[n]) % 2, ("fill_done", 6 * P + {0: 6, 3: 8, 6: 10}[n]))
                    if n % 2:
                        if kind != "C":
                            y_copy(P, n, 1, kind)
                            y_dma(P, n, 0, kind)
                        y_dma(P, n, 1 if kind != "C" else 0, kind)

            iterations(e, body, start, layer)

        def out_projection(o):
            for k in range(KC):
                b = k % 2
                e.wait_ge(S[f"yl_full{b}"], 16 * (4 * o + k // 2 + 1))
                if o == 0:
                    e.activation(YH[:, k, :], YL[:, b, :], ACT.Copy).then_inc(S["yhi_done"], 1)
                else:
                    if k >= 2:
                        e.wait_ge(S["ynorm_done"], k - 1)
                    e.activation(SQ[:, b, :], YL[:, b, :], ACT.Square).then_inc(S["ysq_done"], 1)
                    e.wait_ge(S["yssq_done"], k + 1)
                    e.activation(SQ[:, b, :], banks(SSQ_BANK, 2), ACT.Sqrt, scale=1.0 / 128,
                                 bias=EPS[:, 1:2]).then_inc(S["ysqrt_done"], 1)
                    e.wait_ge(S["ynorm_done"], k + 1)
                    e.activation(YH[:, k, :], YL[:, b, :], ACT.Copy).then_inc(S["yhi_done"], 1)
            N = 2 * o + 1
            e.wait_ge(S["fill_done"], 48 * (o + 1))
            with e.Fori(0, KC // 2) as i:
                for b in range(2):
                    j = 2 * i + b
                    w_split(W_OUT[o] + j + 1, (b + 1) % 2, ("op_done", 1 + 16 * o + 2 * j))
                    e.wait_ge(S["op_free"], 16 * o + 2 * j + 2 + 4)
                    prep_chunk(N, j, b)
            root(N)

        def ffn(n):
            def body(t, first=False, last=False, final=False):
                TT = FT * n + t
                if not first:
                    e.wait_ge(S["d_full"], 16 * TT)
                    e.wait_ge(S["d_done"], 1 + 16 * (TT - 1))
                    e.activation(DS[:, 0, :], DR[:, :], ACT.Copy).then_inc(S["d_hi"], 1)
                    e.wait_ge(S["prod_done"], TT)
                    e.activation(AH[:, :], PROD[:, :], ACT.Copy).then_inc(S["ahi_done"], 1)
                if not last:
                    w_split(W_FFN[n] + 2 * t + 1, 1, ("op_done", 1 + 16 * (n + 1)) if first else ("u_done", TT))
                    e.wait_ge(S["gmul_done"], TT + 1)
                    e.activation(SIL[:, :], banks(G_BANK, 2), ACT.Silu).then_inc(S["sil_done"], 1)
                    if not final:
                        w_split(W_FFN[n] + 2 * t + 2, 0, ("g_done", TT + 1))

            body(0, first=True)
            with e.Fori(1, FT - 1) as t:
                body(t)
            body(FT - 1, final=n == 1)
            body(FT, last=True)
            N = 2 * n + 2
            for j in range(KC):
                e.wait_ge(S["d_free"], 4 + 16 * (FT * (n + 1) - 1) + 2 * j + 2)
                prep_chunk(N, j, j % 2)
            root(N)

        w_split(0, 0)
        for name in ("y_out0", "y_out1"):
            e.sem_inc(S[name], 1)
        e.wait_ge(S["lam_ready"], 2)
        e.activation(NEGLAM[:, 0:2], NEGLAM[:, 2:4], ACT.Exp).then_inc(S["lam_ready"], 1)
        e.wait_ge(S["gains_full"], 48)
        e.wait_ge(S["ones_ready"], 3)
        for j in range(KC):
            e.wait_ge(S[f"x_full{j // 2}"], 16)
            prep_chunk(0, j, j % 2)
        root(0)
        attention(0)
        out_projection(0)
        ffn(0)
        attention(1)
        out_projection(1)
        ffn(1)

    def dve_program(e):
        def w_split(w, slot):
            for x in range(2):
                e.wait_ge(S["w_hi"], 2 * w + x + 1)
                c = 512 * x
                e.tensor_tensor(WS[:, slot, 1, c:c + 512], WR[:, x, :], f(WS[:, slot, 0, c:c + 512]),
                                ALU.subtract).then_inc(S["w_lo"], 1)

        def zero_acc(N):
            if N:
                e.wait_ge(S["ssq_done"], N)
            e.memset(ACC[:, :], 0.0).then_inc(S["acc_zero"], 1)

        def prep_chunk(N, j, b):
            e.wait_ge(S["sq_done"], 8 * N + j + 1)
            e.wait_ge(S["acc_zero"], N + 1)
            if not (isinstance(j, int) and 8 * N + j == 0):
                e.wait_ge(S["sadd"], 8 * N + j)
            e.tensor_tensor(ACC[:, :], ACC[:, :], SQ[:, b, :], ALU.add).then_inc(S["sadd"], 1)
            if N < 4:
                e.wait_ge(S["xhi_done"], 8 * N + j + 1)
                e.scalar_tensor_tensor(out=HL[:, j, :], in0=X[:, j, :], scalar=GAIN[:, N, bass.ds(j, 1)],
                                       in1=f(HH[:, j, :]), op0=ALU.mult, op1=ALU.subtract).then_inc(S["xlo_done"], 1)

        def root(N):
            e.wait_ge(S["sqrt_done"], N + 1)
            e.reciprocal(RSTD[:, :], RSTD[:, :]).then_inc(S["rstd_done"], 1)
            e.wait_ge(S["rstd_done"], N + 1)

        def evac(P, par, k, layer):
            e.wait_ge(S["fill_done"], 6 * P + k + 1)
            half = k % 2
            c = 512 * half
            ps = PS[:, FILL_BANK, :]
            r = RSTD[:, c:c + 512]
            if k < 2:
                e.tensor_tensor(QR[:, par, c:c + 512], ps, r, ALU.mult).then_inc(S["fill_evac"], 1)
            elif k >= 4:
                e.wait_ge(S["tv_done"], 2 * P + 2)
                e.scalar_tensor_tensor(out=QR[:, par, c:c + 512], in0=ps, scalar=-DH ** -0.5, in1=r,
                                       op0=ALU.mult, op1=ALU.mult).then_inc(S["fill_evac"], 1)
            else:
                e.tensor_tensor(ps, ps, r, ALU.mult).then_inc(S["kmul_done"], 1)
                e.wait_ge(S["khi_done"], 4 * P + 2 * half + 2)
                e.tensor_tensor(KS[64:128, par, 0, c:c + 512], ps[0:64], f(KS[0:64, par, 0, c:c + 512]), ALU.subtract)
                e.tensor_tensor(KS[0:64, par, 1, c:c + 512], ps[64:128], f(KS[64:128, par, 1, c:c + 512]),
                                ALU.subtract).then_inc(S["fill_evac"], 1)

        def vlo(P, par, vv, kind):
            e.wait_ge(S["vhi_done"], 2 * P + vv + 1)
            if kind == "C":
                v = VS[:, par, 4 * vv:4 * vv + 4, :]
                dst, high = v[:, :, 128:256], v[:, :, 0:128]
                src = PS[:, PV_BANK, :].rearrange("p (k d) -> p k d", k=4)
            else:
                v = VS[:, par, 4 * vv:4 * vv + 4, :].rearrange("p k (m s d) -> p k m s d", m=2, s=2)
                dst, high = v[:, :, :, 1, :], v[:, :, :, 0, :]
                src = PS[:, PV_BANK, :].rearrange("p (k m d) -> p k m d", k=4, m=2)
            e.tensor_tensor(dst, src, f(high), ALU.subtract).then_inc(S["vlo_done"], 1)

        def xy(P, par, n):
            e.wait_ge(S["fill_evac"], 6 * P + (5 if n < 4 else 6))
            e.wait_ge(S["qk_done"], 1 + 16 * P + 2 * n)
            q = QR[:, par, 128 * n:128 * n + 128]
            e.tensor_copy(XY[64:128, 0, :], q[0:64])
            e.tensor_copy(XY[0:64, 1, :], q[64:128])
            e.wait_ge(S["xy_act"], 16 * P + 2 * n + 2)
            e.tensor_tensor(XY[0:64, 2, :], q[0:64], f(XY[0:64, 0, :]), ALU.subtract)
            e.tensor_tensor(XY[64:128, 3, :], q[64:128], f(XY[64:128, 1, :]), ALU.subtract).then_inc(S["xy_dve"], 1)

        def ttr(P, par, n, m, kind):
            k0, nk = key_tiles(kind, n)
            e.wait_ge(S["qk_done"], 1 + 16 * P + 2 * n + m + 1)
            c = bias_start(kind, n)
            t = (E0[:, 0:128 * nk] if m == 0 else E1[:, n % 2, 0:128 * nk])
            e.sem_inc(S["dve_passed"], 1)
            e.tensor_tensor_reduce(out=t, in0=banks(S_BANK[m], 2)[:, 0:128 * nk],
                                   in1=BIAS[:, par, m if kind != "C" else 0, c:c + 128 * nk],
                                   scale=1.0, scalar=3e38, op0=ALU.add, op1=ALU.min,
                                   accum_out=ST[:, n % 2, m:m + 1]).then_inc(S["ttr_done"], 1)

        def recip(P, n, m):
            e.wait_ge(S["exp_done"], 16 * P + 2 * n + m + 1)
            e.reciprocal(ST[:, n % 2, 4 + m:5 + m], ST[:, n % 2, 2 + m:3 + m]).then_inc(S["rec_done"], 1)

        def norm0(P, n, kind):
            k0, nk = key_tiles(kind, n)
            e.wait_ge(S["rec_done"], 16 * P + 2 * n + 1)
            e.tensor_scalar(E0[:, 0:128 * nk], E0[:, 0:128 * nk], ST[:, n % 2, 4:5], None,
                            ALU.mult).then_inc(S["p0_ready"], 1)

        def factors(P, n):
            e.wait_ge(S["exp_done"], 16 * P + 2 * n + 2)
            e.reciprocal(ST[:, n % 2, 4:6], ST[:, n % 2, 2:4]).then_inc(S["rec_done"], 1)
            e.wait_ge(S["rec_done"], 128 + 8 * P + n + 1 - 64)
            e.tensor_tensor(ST[:, n % 2, 6:7], ST[:, n % 2, 5:6], NEGLAM[:, 2:3], ALU.mult).then_inc(S["c1_ready"], 1)

        def combine(P, n):
            e.wait_ge(S["escaled"], 8 * P + n + 1 - 64)
            e.scalar_tensor_tensor(out=E0[:, :], in0=E0[:, :], scalar=ST[:, n % 2, 4:5], in1=E1[:, n % 2, :],
                                   op0=ALU.mult, op1=ALU.add).then_inc(S["p0_ready"], 1)

        def lo(P, n, m, kind):
            k0, nk = key_tiles(kind, n)
            b = m if kind != "C" else (n // 2) % 2
            e.wait_ge(S["hi_done"], t_count(P, n, m, kind))
            c = 128 * (n % 2)
            e.tensor_tensor(AT[:, b, k0:k0 + nk, 1, c:c + 128],
                            banks(T_BANK, 2)[:, 0:128 * nk].rearrange("p (k q) -> p k q", k=nk),
                            f(AT[:, b, k0:k0 + nk, 0, c:c + 128]), ALU.subtract).then_inc(S["lo_done"], 1)

        def y_add(P, n, m, kind):
            if kind == "C":
                b = (n // 2) % 2
                e.wait_ge(S["pv_done"], unit(P, n, m, kind) + 3)
                e.wait_ge(S[f"y_out{b}"], 1 + 16 * (32 + 2 * (P - 8) + n // 4))
                e.tensor_copy(YS[:, b, :], PS[:, PV_BANK, 0:256]).then_inc(S["y_done"], 1)
            else:
                e.wait_ge(S["y_copy"], unit(P, n, m, kind) + 1)
                e.tensor_tensor(YS[0:64, m, :], PS[0:64, PV_BANK, 0:256], YS[0:64, m, :],
                                ALU.add).then_inc(S["y_done"], 1)

        def bias_ready(P, par, kind):
            e.wait_ge(S[f"bias_full{par}"], 8 * P - 8 * par + 16)

        def negate(P, par):
            bias_ready(P, par, "B")
            for m in range(2):
                e.tensor_scalar(BIAS[:, par, m, 0:TAB_B], BIAS[:, par, m, 0:TAB_B], -1.0, None,
                                ALU.mult).then_inc(S["bneg_done"], 1)

        def attention(layer):
            P0, kind = 8 * layer, "AC"[layer]
            w0 = strip_of(P0, layer)
            w_split(w0 + 1, 1)
            if layer:
                e.wait_ge(S["x_saved"], 16)
            e.memset(f(XY[:, 2:4, :]), 0.0).then_inc(S["xy_zero"], 1)
            e.wait_ge(S["xy_zero"], layer + 1)
            evac(P0, 0, 0, layer)
            w_split(w0 + 2, 0)
            evac(P0, 0, 1, layer)
            vlo(P0, 0, 0, kind)
            evac(P0, 0, 2, layer)
            vlo(P0, 0, 1, kind)
            evac(P0, 0, 3, layer)
            evac(P0, 0, 4, layer)
            w_split(w0 + 3, 1)
            evac(P0, 0, 5, layer)

            def softmax(P, par, n, kind):
                ttr(P, par, n, 0, kind)
                ttr(P, par, n, 1, kind)

            def start(P, par, kind):
                bias_ready(P, par, kind)
                if kind == "B":
                    negate(P, par)
                    e.wait_ge(S["bneg_done"], 2 * (P - 4) + 2)
                xy(P, par, 0)
                softmax(P, par, 0, kind)
                xy(P, par, 1)
                if kind == "C":
                    factors(P, 0)
                    combine(P, 0)
                else:
                    recip(P, 0, 0)
                    norm0(P, 0, kind)
                    recip(P, 0, 1)

            def body(P, par, kind, nxt, looks):
                w = strip_of(P, layer)
                for n in range(NQ):
                    go = n < NQ - 1 or looks
                    Pn, nn, parn = (P, n + 1, par) if n < NQ - 1 else (P + 1, 0, 1 - par)
                    if n in EVAC_AT and nxt:
                        evac(P + 1, 1 - par, EVAC_AT[n], layer)
                    lo(P, n, 0, kind)
                    if go:
                        if n == NQ - 1:
                            bias_ready(P + 1, 1 - par, kind)
                            if kind == "B":
                                e.wait_ge(S["bneg_done"], 2 * (P + 1 - 4) + 2)
                        softmax(Pn, parn, nn, kind)
                    if n < NQ - 2:
                        xy(P, par, n + 2)
                    elif looks:
                        xy(P + 1, 1 - par, n - 6)
                    if kind == "C":
                        if go:
                            factors(Pn, nn)
                    else:
                        if go:
                            recip(Pn, nn, 0)
                            norm0(Pn, nn, kind)
                        lo(P, n, 1, kind)
                        if go:
                            recip(Pn, nn, 1)
                    if nxt and n in TV_AT:
                        vlo(P + 1, 1 - par, TV_AT[n], kind)
                    if kind == "C" and go:
                        combine(Pn, nn)
                    if nxt == "B" and n == 3:
                        negate(P + 1, 1 - par)
                    if n % 2:
                        y_add(P, n, 0, kind)
                    if nxt and n in SPLIT_AT:
                        w_split(w + SPLIT_AT[n], (par + SPLIT_AT[n]) % 2)
                    if n % 2 and kind != "C":
                        y_add(P, n, 1, kind)
                if nxt:
                    evac(P + 1, 1 - par, 5, layer)

            iterations(e, body, start, layer)

        def out_projection(o):
            for k in range(KC):
                b = k % 2
                if o == 1:
                    e.wait_ge(S["ysqrt_done"], k + 1)
                    e.reciprocal(SQ[:, b, :], SQ[:, b, :]).then_inc(S["yrec_done"], 1)
                    e.wait_ge(S["yrec_done"], k + 1)
                    e.scalar_tensor_tensor(out=YL[:, b, :], in0=YL[:, b, :], scalar=SUBG[:, 1:2], in1=SQ[:, b, :],
                                           op0=ALU.mult, op1=ALU.mult).then_inc(S["ynorm_done"], 1)
                e.wait_ge(S["yhi_done"], 8 * o + k + 1)
                e.tensor_tensor(YO[:, k, :], YL[:, b, :], f(YH[:, k, :]), ALU.subtract).then_inc(S["ylo_done"], 1)
            N = 2 * o + 1
            zero_acc(N)
            for c in range(4):
                e.wait_ge(S[f"x_full{c}"], 16 * (o + 2))
            with e.Fori(0, KC // 2) as i:
                for b in range(2):
                    j = 2 * i + b
                    w_split(W_OUT[o] + j + 1, (b + 1) % 2)
                    for h in range(2):
                        e.wait_ge(S["op_done"], 1 + 16 * o + 2 * j + h + 1)
                        xs = X[:, j, 512 * h:512 * h + 512]
                        e.tensor_tensor(xs, PS[:, 2 * b + h, :], xs, ALU.add).then_inc(S["op_free"], 1)
                    prep_chunk(N, j, b)
            root(N)

        def ffn(n):
            def body(t, first=False, last=False, final=False):
                TT = FT * n + t
                if not first:
                    e.wait_ge(S["u_done"], TT)
                    e.tensor_tensor(UT[:, :], banks(U_BANK, 2), RSTD[:, :], ALU.mult).then_inc(S["umul_done"], 1)
                    e.wait_ge(S["d_hi"], TT)
                    e.tensor_tensor(DS[:, 1, :], DR[:, :], f(DS[:, 0, :]), ALU.subtract).then_inc(S["d_lo"], 1)
                    e.wait_ge(S["sil_done"], TT)
                    e.wait_ge(S["umul_done"], TT)
                    e.tensor_tensor(PROD[:, :], SIL[:, :], UT[:, :], ALU.mult).then_inc(S["prod_done"], 1)
                    e.wait_ge(S["ahi_done"], TT)
                    e.tensor_tensor(AL[:, :], PROD[:, :], f(AH[:, :]), ALU.subtract).then_inc(S["alo_done"], 1)
                if not last:
                    w_split(W_FFN[n] + 2 * t + 1, 1)
                for ev in range(16):
                    if not first:
                        e.wait_ge(S["d_done"], 1 + 16 * (TT - 1) + ev + 1)
                        xs = X[:, ev // 2, 512 * (ev % 2):512 * (ev % 2) + 512]
                        e.tensor_tensor(xs, PS[:, D_BANK + ev % 4, :], xs, ALU.add).then_inc(S["d_free"], 1)
                    if ev == 5 and not last:
                        e.wait_ge(S["g_done"], TT + 1)
                        g = banks(G_BANK, 2)
                        e.tensor_tensor(g, g, RSTD[:, :], ALU.mult).then_inc(S["gmul_done"], 1)
                    if ev == 8 and not last and not final:
                        w_split(W_FFN[n] + 2 * t + 2, 0)

            body(0, first=True)
            with e.Fori(1, FT - 1) as t:
                body(t)
            body(FT - 1, final=n == 1)
            body(FT, last=True)
            N = 2 * n + 2
            zero_acc(N)
            for j in range(KC):
                prep_chunk(N, j, j % 2)
            root(N)

        w_split(0, 0)
        e.wait_ge(S["gains_full"], 48)
        e.tensor_tensor(LP[:, 0, :], LV[:, 0, :], LV[:, 1, :], ALU.mult).then_inc(S["consts_ready"], 1)
        e.tensor_tensor(LP[:, 1, :], LV[:, 2, :], LV[:, 3, :], ALU.mult).then_inc(S["consts_ready"], 1)
        e.wait_ge(S["consts_ready"], 2)
        e.reduce_sum(NEGLAM[:, 2:3], LP[:, 0, :], axis=mybir.AxisListType.X).then_inc(S["lam_ready"], 1)
        e.reduce_sum(NEGLAM[:, 3:4], LP[:, 1, :], axis=mybir.AxisListType.X).then_inc(S["lam_ready"], 1)
        e.tensor_scalar(SUBG[:, 1:2], SUBG[:, 0:1], 1.0 - LAM_INIT, None, ALU.mult).then_inc(S["consts_ready"], 1)
        e.wait_ge(S["lam_ready"], 3)
        e.tensor_tensor(NEGLAM[:, 3:4], NEGLAM[:, 1:2], NEGLAM[:, 0:1], ALU.subtract).then_inc(S["consts_ready"], 1)
        e.wait_ge(S["consts_ready"], 4)
        e.tensor_scalar(NEGLAM[:, 2:3], NEGLAM[:, 3:4], -LAM_INIT, None, ALU.add).then_inc(S["consts_ready"], 1)
        for name in ("ttr_done", "y_done", "lo_done", "d_lo"):
            e.sem_inc(S[name], 1)
        e.sem_inc(S["op_free"], 4)
        e.sem_inc(S["d_free"], 4)
        zero_acc(0)
        for j in range(KC):
            prep_chunk(0, j, j % 2)
        root(0)
        attention(0)
        out_projection(0)
        ffn(0)
        attention(1)
        out_projection(1)
        ffn(1)
        for k in range(KC):
            e.scalar_tensor_tensor(out=X[:, k, :], in0=X[:, k, :], scalar=GAIN[:, 4, k:k + 1], in1=RSTD[:, :],
                                   op0=ALU.mult, op1=ALU.mult).then_inc(S["out_ready"], 1)

    def pe_program(e):
        def three(ps, wh, wl, xh, xl, start, stop):
            e.matmul(ps, wh, xh, start=start, stop=False)
            e.matmul(ps, wh, xl, start=False, stop=False)
            return e.matmul(ps, wl, xh, start=False, stop=stop)

        def ssq(N):
            e.wait_ge(S["sadd"], 8 * N + 8)
            e.wait_ge(S["ones_ready"], 1)
            for h in range(2):
                last = e.matmul(PS[:, SSQ_BANK + h, :], ONES[:, :], ACC[:, 512 * h:512 * h + 512], start=True, stop=True)
            last.then_inc(S["ssq_done"], 1)

        def fill(P, k, a, b, layer, prep=None):
            w = strip_of(P, layer) + k // 2
            h = k % 2
            slot = (fill_par[0] + k // 2) % 2
            if a == 0:
                e.wait_ge(S["fill_evac"], 6 * P + k)
            ps = PS[:, FILL_BANK, :]
            for g in range(a, b):
                c, part = g // 3, g % 3
                if h == 0 and g in (0, 12):
                    e.wait_ge(S["w_lo"], 2 * w + 1 + g // 12)
                if prep is not None and part == 0:
                    e.wait_ge(S["xlo_done"], 8 * prep + c + 1)
                wt = WS[:, slot, 1 if part == 2 else 0, 128 * c:128 * c + 128]
                xt = (HL if part == 1 else HH)[:, c, 512 * h:512 * h + 512]
                last = e.matmul(ps, wt, xt, start=g == 0, stop=g == 23)
            if b == 24:
                last.then_inc(S["fill_done"], 1)

        fill_par = [0]

        def tv(P, par, vv, kind):
            e.wait_ge(S["fill_evac"], 6 * P + vv + 1)
            for k in range(4):
                c = 512 * vv + 128 * k
                last = e.transpose(PS[:, PV_BANK, 128 * k:128 * k + 128], QR[:, par, c:c + 128], IDENT[:, :])
            last.then_inc(S["tv_done"], 1)

        def qk(P, par, n, kind, fresh=False):
            k0, nk = key_tiles(kind, n)
            e.wait_ge(S["xy_dve"], 8 * P + n + 1)
            for m in range(2):
                e.wait_ge(S["ttr_done"], 1 + 16 * P + (0 if fresh else 2 * n + m - 1))
                for c in range(0, nk, 4):
                    wd = 128 * min(4, nk - c)
                    k = 128 * (k0 + c)
                    ps = PS[:, S_BANK[m] + c // 4, 0:wd]
                    e.matmul(ps, XY[:, m, :], KS[:, par, m, k:k + wd], start=True, stop=False)
                    last = e.matmul(ps, XY[:, 2 + m, :], KS[:, par, m, k:k + wd], start=False, stop=True)
                last.then_inc(S["qk_done"], 1)

        def turn(P, n, m, kind):
            k0, nk = key_tiles(kind, n)
            e.wait_ge(S["p0_ready" if m == 0 else "p1_ready"], 8 * P + n + 1)
            e.wait_ge(S["lo_done"], 1 + t_count(P, n, m, kind) - 1)
            src = E0 if m == 0 else E1[:, n % 2, :]
            for k in range(nk):
                last = e.transpose(PS[:, T_BANK + k // 4, 128 * (k % 4):128 * (k % 4) + 128],
                                   src[:, 128 * k:128 * k + 128], IDENT[:, :])
            last.then_inc(S["t_done"], 1)

        def pv(P, par, n, m, kind):
            b = m if kind != "C" else (n // 2) % 2
            u = unit(P, n, m, kind)
            e.wait_ge(S["lo_done"], 1 + t_count(P, n, m, kind))
            e.wait_ge(S["y_done"], 1 + u)
            e.wait_ge(S["vlo_done"], 2 * P + 2)
            a0, na = key_tiles(kind, n - 1)
            b0, nb = key_tiles(kind, n)
            both = list(range(max(a0, b0), min(a0 + na, b0 + nb)))
            tiles = [(k, 0, 256) for k in both]
            tiles += [(k, 0, 128) for k in range(a0, a0 + na) if k not in both]
            tiles += [(k, 128, 256) for k in range(b0, b0 + nb) if k not in both]
            todo = []
            for k, lo_, hi_ in tiles:
                if kind == "C":
                    passes = [(0, 0), (0, 1), (128, 0)]
                    todo += [(VS[:, par, k, v:v + 128], AT[:, b, k, p, lo_:hi_], lo_, hi_) for v, p in passes]
                else:
                    v = VS[:, par, k, 128 * m:128 * m + 128]
                    todo += [(v, AT[:, b, k, p, lo_:hi_], lo_, hi_) for p in range(2)]
            for i, (v, p, lo_, hi_) in enumerate(todo):
                last = e.matmul(PS[:, PV_BANK, lo_:hi_], v, p, start=i == 0, stop=i == len(todo) - 1)
            last.then_inc(S["pv_done"], 1)

        def attention(layer):
            P0, kind, N = 8 * layer, "AC"[layer], 2 * layer
            fill_par[0] = 0
            if layer:
                e.wait_ge(S["d_free"], 4 + 16 * FT)
            fill(P0, 0, 0, 24, layer, prep=N)
            ssq(N)
            fill(P0, 1, 0, 24, layer)
            tv(P0, 0, 0, kind)
            fill(P0, 2, 0, 24, layer)
            e.wait_ge(S["vlo_done"], 2 * P0 + 1)
            tv(P0, 0, 1, kind)
            for k in (3, 4, 5):
                fill(P0, k, 0, 24, layer)

            def start(P, par, kind):
                qk(P, par, 0, kind, fresh=True)

            def body(P, par, kind, nxt, looks):
                fill_par[0] = 1 - par
                for n in range(NQ):
                    turn(P, n, 0, kind)
                    if n < NQ - 1:
                        qk(P, par, n + 1, kind)
                    elif looks:
                        qk(P + 1, 1 - par, 0, kind)
                    k, a, b = FILLS[n]
                    third = (b - a) // 3
                    if nxt:
                        fill(P + 1, k, a, a + third, layer)
                    if kind != "C":
                        turn(P, n, 1, kind)
                    if nxt:
                        fill(P + 1, k, a + third, a + 2 * third, layer)
                    if nxt and n in TV_AT:
                        e.wait_ge(S["y_done"], 1 + unit(P, n, 0, kind))
                        tv(P + 1, 1 - par, TV_AT[n], kind)
                    if n % 2:
                        if nxt and n - 1 in TV_AT:
                            e.wait_ge(S["vlo_done"], 2 * (P + 1) + TV_AT[n - 1] + 1)
                        pv(P, par, n, 0, kind)
                    if nxt:
                        fill(P + 1, k, a + 2 * third, b, layer)
                    if n % 2 and kind != "C":
                        pv(P, par, n, 1, kind)

            iterations(e, body, start, layer)

        def out_projection(o):
            if o == 1:
                for k in range(KC):
                    e.wait_ge(S["ysq_done"], k + 1)
                    if k:
                        e.wait_ge(S["ysqrt_done"], k)
                    for h in range(2):
                        last = e.matmul(PS[:, SSQ_BANK + h, :], ONES[:, :], SQ[:, k % 2, 512 * h:512 * h + 512],
                                        start=True, stop=True)
                    last.then_inc(S["yssq_done"], 1)
            with e.Fori(0, KC // 2) as i:
                for b in range(2):
                    j = 2 * i + b
                    w = W_OUT[o] + j
                    for h in range(2):
                        ps = PS[:, 2 * b + h, :]
                        e.wait_ge(S["op_free"], 16 * o + 2 * j + h + 1)
                        for k in range(KC):
                            if h == 0 and k % 4 == 0:
                                e.wait_ge(S["w_lo"], 2 * w + 1 + k // 4)
                            if h == 0 and b == 0:
                                e.wait_ge(S["ylo_done"], 8 * o + k + 1)
                            last = three(ps, WS[:, b, 0, 128 * k:128 * k + 128], WS[:, b, 1, 128 * k:128 * k + 128],
                                         YH[:, k, 512 * h:512 * h + 512], YO[:, k, 512 * h:512 * h + 512],
                                         k == 0, k == KC - 1)
                        last.then_inc(S["op_done"], 1)

        def ffn(n):
            N = 2 * n + 1

            def body(t, first=False, last=False):
                TT = FT * n + t
                w = W_FFN[n] + 2 * t
                if first:
                    e.wait_ge(S["op_free"], 4 + 16 * (n + 1))
                e_next = 0
                for step in range(16):
                    if not last:
                        gate, h, c0 = step < 8, (step // 4) % 2, 2 * (step % 4)
                        slot = 0 if gate else 1
                        ps = PS[:, (G_BANK if gate else U_BANK) + h, :]
                        if step == 0:
                            e.wait_ge(S["sil_done"], TT)
                        if step == 8:
                            if first:
                                ssq(N)
                            e.wait_ge(S["umul_done"], TT)
                        for c in (c0, c0 + 1):
                            if h == 0 and c % 4 == 0:
                                e.wait_ge(S["w_lo"], 2 * (w + slot) + 1 + c // 4)
                            if first and step < 4:
                                e.wait_ge(S["xlo_done"], 8 * N + c + 1)
                            mm = three(ps, WS[:, slot, 0, 128 * c:128 * c + 128], WS[:, slot, 1, 128 * c:128 * c + 128],
                                       HH[:, c, 512 * h:512 * h + 512], HL[:, c, 512 * h:512 * h + 512],
                                       c == 0, c == KC - 1)
                        if step in (7, 15):
                            mm.then_inc(S["g_done" if gate else "u_done"], 1)
                    if not first and step >= 4:
                        until = 16 if step == 15 else (step - 3) * 16 // 12
                        while e_next < until:
                            ev = e_next
                            if ev == 0:
                                e.wait_ge(S["alo_done"], TT)
                                e.wait_ge(S["d_lo"], 1 + TT)
                                e.wait_ge(S["rstd_done"], N + 1)
                            e.wait_ge(S["d_free"], 16 * (TT - 1) + ev + 1)
                            j, h = ev // 2, ev % 2
                            mm = three(PS[:, D_BANK + ev % 4, :], DS[:, 0, 128 * j:128 * j + 128],
                                       DS[:, 1, 128 * j:128 * j + 128], AH[:, 512 * h:512 * h + 512],
                                       AL[:, 512 * h:512 * h + 512], True, True)
                            mm.then_inc(S["d_done"], 1)
                            e_next += 1

            body(0, first=True)
            with e.Fori(1, FT) as t:
                body(t)
            body(FT, last=True)

        e.wait_ge(S["ident_ready"], 2)
        e.sem_inc(S["pv_done"], 2)
        for name in ("qk_done", "op_done", "d_done"):
            e.sem_inc(S[name], 1)
        attention(0)
        out_projection(0)
        ffn(0)
        attention(1)
        out_projection(1)
        ffn(1)
        ssq(4)

    with nc.Block() as block:
        @block.sync
        def _(e):
            sync_program(e)

        @block.gpsimd
        def _(e):
            pool_program(e)

        @block.scalar
        def _(e):
            act_program(e)

        @block.vector
        def _(e):
            dve_program(e)

        @block.tensor
        def _(e):
            pe_program(e)


def tables():
    p = np.arange(128)[:, None]
    d = np.abs(np.arange(BIAS_W)[None, :] - 128 * (NQ - 1) - p)
    slopes = np.exp2(-np.arange(1, 9, dtype=np.float64))
    count = sum(((d % dil == 0) & (d <= win // 2)).astype(int) for win, dil in ((128, 1), (512, 4), (2048, 16)))
    fixed = np.where(count > 0, -np.log(np.maximum(count, 1)), BIG)
    a = slopes[:, None, None] * d[None] + fixed[None]
    a = a.reshape(4, 2, 128, BIAS_W).transpose(0, 2, 1, 3)
    c = slopes[:, None, None] * d[None]
    return a.astype(np.float32), c.astype(np.float32)


def table_b_index():
    par, col = np.divmod(np.arange(128), GRID)
    first = np.clip(col - COLS // 2, 0, GRID - COLS)
    k = np.arange(GRID)
    inside = (k >= first[:, None]) & (k < first[:, None] + COLS)
    dc = k[None] - col[:, None] + COLS - 1
    rows = []
    for start, n, window in ((-6, EDGE_ROWS, None), (-4, MID_ROWS, (-4, 3))):
        for u in range(start, start + n):
            dr = u - par + ROWS - 1
            ok = (dr >= 0) & (dr < 2 * ROWS - 1)
            if window:
                ok &= (u - par >= window[0]) & (u - par <= window[1])
            rows.append(np.where(ok[:, None] & inside, dr[:, None] * (2 * COLS - 1) + dc, -1))
    return np.concatenate(rows, axis=1)


def strips(w, order):
    w = w.reshape(KC, 128, -1)
    s = np.stack([w[:, :, c:c + 128] for c in order])
    s = s.reshape(len(order), 2, 4, 128, 128).transpose(0, 1, 3, 2, 4)
    return s.reshape(len(order), 2, 128, 512)


def kernel(x, a0_norm, a0_w_in, a0_w_out, a0_rpb, f0_norm, f0_w_gate, f0_w_up, f0_w_down,
           a1_norm, a1_w_qkv, a1_w_out, a1_lam_q1, a1_lam_k1, a1_lam_q2, a1_lam_k2, a1_subln,
           f1_norm, f1_w_gate, f1_w_up, f1_w_down, final_norm):
    import concourse.bacc as bacc
    from concourse.bass_utils import run_bass_kernel_spmd

    n = lambda a: np.asarray(a)
    order0 = [base + 128 * p + off for base in (0, 1536) for p in range(4) for off in (1024, 512, 0)]
    order1 = [128 * h + off for h in range(8) for off in (2048, 1024, 0)]

    def gate_up(g, u):
        s = np.stack([strips(n(g), range(0, F, 128)), strips(n(u), range(0, F, 128))], axis=1)
        return s.reshape(2 * FT, 2, 128, 512)

    cols = list(range(0, D, 128))
    wstrips = np.concatenate([
        strips(n(a0_w_in), order0), strips(n(a0_w_out), cols), gate_up(f0_w_gate, f0_w_up),
        strips(n(a1_w_qkv), order1), strips(n(a1_w_out), cols), gate_up(f1_w_gate, f1_w_up)])
    wdown = np.concatenate([n(f0_w_down), n(f1_w_down)]).reshape(2 * FT, 128, D)
    gains = np.stack([n(g).reshape(KC, 128).T for g in (a0_norm, f0_norm, a1_norm, f1_norm, final_norm)], axis=1)
    lams = np.stack([n(a1_lam_q1), n(a1_lam_k1), n(a1_lam_q2), n(a1_lam_k2)])
    ali_a, ali_c = tables()
    index = table_b_index()
    rpb = n(a0_rpb).reshape(8, -1)
    tab_b = np.where(index < 0, np.float32(-BIG), rpb[:, np.maximum(index, 0)]).astype(np.float32)
    tab_b = tab_b.reshape(4, 2, 128, TAB_B).transpose(0, 2, 1, 3)
    list_a = np.zeros((5, 128, 2, BIAS_W), np.float32)
    list_a[:4] = ali_a
    list_a[4, :, :, :TAB_B] = tab_b[0]

    arrays = {
        "x": n(x).reshape(T, KC, 128).transpose(2, 1, 0), "wstrips": wstrips, "wdown": wdown, "gains": gains,
        "subln": n(a1_subln).reshape(128, 1), "lams": lams, "ali_a": list_a, "ali_c": ali_c, "tab_b": tab_b,
    }
    arrays = {k: np.ascontiguousarray(v) for k, v in arrays.items()}
    nc = bacc.Bacc("TRN2", target_bir_lowering=False, num_devices=1)
    aps = [nc.dram_tensor(k, list(v.shape), mybir.dt.from_np(v.dtype), kind="ExternalInput").ap()
           for k, v in arrays.items()]
    out = nc.dram_tensor("out", [128, KC, T], mybir.dt.float32, kind="ExternalOutput").ap()
    build(nc, *aps, out)
    r = run_bass_kernel_spmd(nc, [arrays], core_ids=[0])
    y = np.asarray(r.results[0]["out"])
    return y.transpose(2, 1, 0).reshape(1, T, D)
```

```python
import math

import numpy as np
import concourse.bass as bass
from concourse import mybir

D = 1024
T = 1024
KC = D // 128
DH = 64
F = 2816
FT = F // 128
NP = 8
NQ = T // 128
RMS_EPS = 1e-6
SUBLN_EPS = 1e-5
LAM_INIT = 0.8 - 0.6 * math.exp(-0.3)
GRID, ROWS, COLS = 64, 8, 16
BIG = 1e30
BIAS_W = T + (NQ - 1) * 128
EDGE_ROWS, MID_ROWS = 14, 10
TAB_B = (EDGE_ROWS + MID_ROWS) * GRID

PROJ = 3 * NP
W_ATTN = [0, PROJ + KC + 2 * FT]
W_OUT = [w + PROJ for w in W_ATTN]
W_FFN = [w + KC for w in W_OUT]
N_STRIPS = 2 * (PROJ + KC + 2 * FT)


def key_tiles(kind, n):
    if kind != "B":
        return 0, NQ
    lo = max(0, min(2 * n - ROWS // 2, 2 * NQ - ROWS))
    hi = max(0, min(2 * n + 1 - ROWS // 2, 2 * NQ - ROWS)) + ROWS
    return lo // 2, (hi + 1) // 2 - lo // 2


def bias_start(kind, n):
    if kind != "B":
        return 128 * (NQ - 1 - n)
    first = 2 * key_tiles("B", n)[0] - 2 * n
    if key_tiles("B", n)[1] == 5:
        return (EDGE_ROWS + first + 4) * GRID
    return (first + 6) * GRID


def build(nc, x_in, wstrips, wdown, gains, subln, lams, ali_a, ali_c, tab_b, out):
    f32, f32r = mybir.dt.float32, mybir.dt.float32r
    ALU, ACT = mybir.AluOpType, mybir.ActivationFunctionType

    place = [-(-nc.sbuf_base // 64) * 64]

    def sb(name, shape, dt=f32):
        size = int(np.prod(shape[1:])) * 4
        t = nc.alloc_sbuf_tensor_at(name, shape, dt, offset=place[0])
        place[0] += -(-size // 32) * 32
        return t

    products = place[0]
    HH = sb("HH", [128, KC, T], f32r)
    HL = sb("HL", [128, KC, T], f32r)
    RSTD = sb("RSTD", [128, T])
    WS = sb("WS", [128, 2, 2, 1024], f32r)
    WR = sb("WR", [128, 2, 512])
    IDENT = sb("IDENT", [128, 128])
    ONES = sb("ONES", [128, 128])
    GAIN = sb("GAIN", [128, 5, KC])
    SUBG = sb("SUBG", [128, 2])
    NEGLAM = sb("NEGLAM", [128, 4])
    EPS = sb("EPS", [128, 2])
    RT = sb("RT", [128, KC, NQ])
    ST = sb("ST", [128, 2, 8])
    region = place[0]

    XY = sb("XY", [128, 4, 128], f32r)
    KS = sb("KS", [128, 2, 2, T], f32r)
    QR = sb("QR", [128, 2, T])
    VS = sb("VS", [128, 2, NQ, 256], f32r)
    BIAS = sb("BIAS", [128, 2, 2, BIAS_W])
    AT = sb("AT", [128, 2, NQ, 2, 256], f32r)
    E0 = sb("E0", [128, T])
    E1 = sb("E1", [128, 2, T])
    YS = sb("YS", [128, 2, 256])
    assert place[0] <= nc.sbuf_usable_end
    place[0] = region
    X = sb("X", [128, KC, T])
    SQ = sb("SQ", [128, 2, T])
    ACC = sb("ACC", [128, T])
    shared = place[0]
    LV = sb("LV", [128, 4, DH])
    LP = sb("LP", [128, 2, DH])
    place[0] = shared
    FH = sb("FH", [128, KC, T], f32r)
    FL = sb("FL", [128, KC, T], f32r)
    AH = sb("AH", [128, T], f32r)
    AL = sb("AL", [128, T], f32r)
    assert place[0] <= nc.sbuf_usable_end
    place[0] = products
    YQ = sb("YQ", [128, KC, T])
    Y = sb("Y", [128, KC, T])
    place[0] = products
    DR = sb("DR", [128, 1024])
    SIL = sb("SIL", [128, T])
    UT = sb("UT", [128, T])
    PROD = sb("PROD", [128, T])
    place[0] = products + 4 * T * (2 * KC - 2)
    DS = sb("DS", [128, 2, 1024], f32r)

    y_dram = nc.dram_tensor("y_scratch", [KC, 128, T], f32, kind="Internal").ap()
    x_dram = nc.dram_tensor("x_scratch", [128, KC, T], f32, kind="Internal").ap()

    PS = nc.alloc_psum_tensor("PS", [128, 8, 512], f32)
    S_BANK, T_BANK, PV_BANK, FILL_BANK = (0, 2), 4, 6, 7
    G_BANK, U_BANK, D_BANK, SSQ_BANK = 0, 2, 4, 4

    def banks(a, n, w=512):
        return PS[:, a:a + n, 0:w].rearrange("p a b -> p (a b)")

    def k_full(layer, bank):
        return PS[:, bank, :] if layer == 0 else BIAS[:, 1, 1, 0:512]

    def e_tile(kind, n, m, w=T):
        if m:
            return E1[:, n % 2, 0:w]
        if kind == "C" and n % 2:
            return BIAS[:, 0, 1, 0:w]
        return E0[:, 0:w]

    def f(ap):
        return ap.bitcast(f32)

    S = {}
    for name in ("ones_ready ident_ready gains_full consts_ready lam_ready acc_zero acc_zeroed "
                 "raw_full0 raw_full1 w_hi w_lo "
                 "x_full0 x_full1 x_full2 x_full3 x_saved "
                 "sq_done xhi_done xlo_done sadd ssq_done sqrt_done rinv_done spread_done rstd_done "
                 "fill_done fill_evac kmul_done khi_done tv_done vhi_done vlo_done "
                 "xy_act xy_dve bias_full0 bias_full1 bneg_done qk_done ttr_done exp_done rec_done "
                 "p0_ready p1_ready c1_ready escaled t_done hi_done lo_done pv_done y_copy y_done "
                 "y_out0 y_out1 yl_full0 yl_full1 yl_full2 yl_full3 yl_full4 yl_full5 yl_full6 yl_full7 "
                 "yhi_done ylo_done ysq_done yssq_done ysqrt_done yrec_done yspread_done ynorm_done "
                 "dve_passed pool_passed op_done op_free g_done u_done gmul_done sil_done umul_done "
                 "prod_done ahi_done alo_done "
                 "d_full d_hi d_lo d_done d_free xy_zero out_ready out_full").split():
        S[name] = nc.alloc_semaphore(name)

    def unit(P, n, m, kind):
        return 8 * P + 2 * (n // 2) + m if kind != "C" else 64 + 4 * (P - 8) + n // 2

    def t_count(P, n, m, kind):
        return 16 * P + 2 * n + m + 1 if kind != "C" else 128 + 8 * (P - 8) + n + 1

    def iterations(eng, body, head, layer):
        if layer == 0:
            with eng.Fori(0, 2) as i:
                head(2 * i, 0, "A")
                body(2 * i, 0, "A", "A", True)
                body(2 * i + 1, 1, "A", "AB", False)
            head(4, 0, "B")
            for P in range(4, 8):
                body(P, P % 2, "B", "B" if P < 7 else None, P < 7)
        else:
            head(8, 0, "C")
            with eng.Fori(0, 3) as i:
                for par in range(2):
                    body(8 + 2 * i + par, par, "C", "C", True)
            body(14, 0, "C", "C", True)
            body(15, 1, "C", None, False)

    def thirds(k, a, b):
        c = (b - a) // 3
        return [(k, a, a + c), (k, a + c, a + 2 * c), (k, a + 2 * c, b)]

    FILLS_AB = [thirds(0, 0, 24), thirds(1, 0, 12), [(1, 12, 24), None, (2, 0, 12)], thirds(2, 12, 24),
                thirds(3, 0, 24), thirds(4, 0, 12), [(4, 12, 24), None, (5, 0, 12)], thirds(5, 12, 24)]
    FILLS_C = [thirds(0, 0, 24), thirds(1, 0, 24), thirds(2, 0, 12), [(2, 12, 24), None, (3, 0, 8)],
               thirds(3, 8, 24), thirds(4, 0, 20), [(4, 20, 24), None, (5, 0, 6)], [None, (5, 6, 15), (5, 15, 24)]]
    FILLS = {"A": FILLS_AB, "B": FILLS_AB, "C": FILLS_C}
    EVAC_START_AB, EVAC_START_C = {1: 0, 4: 2, 5: 3}, {1: 0, 2: 1, 5: 3}
    EVAC_MID_AB, EVAC_MID_C = {2: 1, 6: 4}, {3: 2, 6: 4}
    EVAC_START = {"A": EVAC_START_AB, "B": EVAC_START_AB, "C": EVAC_START_C}
    EVAC_MID = {"A": EVAC_MID_AB, "B": EVAC_MID_AB, "C": EVAC_MID_C}
    TV_AT_AB, TV_AT_C = {2: 0, 4: 1}, {3: 0, 5: 1}
    TV_AT = {"A": TV_AT_AB, "B": TV_AT_AB, "C": TV_AT_C}
    SPLIT_AT = {0: 4, 3: 5, 6: 6}
    SPLIT_USED = {0: 6, 3: 8, 6: 10}
    FIRST_BANKS = [3, 2, 1, 0, 7, 3]
    EARLY = 5

    def strip_of(P, layer):
        return 3 * P if layer == 0 else 3 * P + (W_ATTN[1] - 24)

    def sync_program(e):
        def raw(w):
            for x in range(2):
                if not (isinstance(w, int) and w == 0):
                    e.wait_ge(S["w_lo"], 2 * w + x - 1)
                e.dma_start(WR[:, x, :], wstrips[w, x]).then_inc(S[f"raw_full{x}"], 16)

        def load_x(src):
            for c in range(4):
                e.dma_start(X[:, 2 * c:2 * c + 2, :], src[:, 2 * c:2 * c + 2, :]).then_inc(S[f"x_full{c}"], 16)

        def bias(P, par, kind):
            e.wait_ge(S["ttr_done"], 1 + 16 * (P - 1) if not isinstance(P, int) or P else 1)
            if kind == "C":
                e.dma_start(BIAS[:, par, 0, :], ali_c[P - 8]).then_inc(S[f"bias_full{par}"], 16)
            else:
                src, w = (ali_a, BIAS_W) if kind == "A" else (tab_b, TAB_B)
                pair = P if kind == "A" else P - 4
                e.dma_start(BIAS[:, par, :, 0:w], src[pair]).then_inc(S[f"bias_full{par}"], 16)

        def attention(layer):
            P0 = 8 * layer
            kind = "AC"[layer]
            w0 = strip_of(P0, layer)
            raw(w0 + 2)
            e.wait_ge(S["rstd_done"], 2 * layer + 1)
            bias(P0, 0, kind)
            raw(w0 + 3)
            raw(w0 + 4)

            def body(P, par, kind, nxt, looks):
                if nxt is None:
                    return
                w = strip_of(P, layer)
                raw(w + 5)
                if nxt != "AB":
                    bias(P + 1, 1 - par, nxt)
                raw(w + 6)
                raw(w + 7)

            if layer == 0:
                with e.Fori(0, 2) as i:
                    for par in range(2):
                        P = 2 * i + par
                        w = strip_of(P, layer)
                        raw(w + 5)
                        e.wait_ge(S["ttr_done"], 1 + 16 * P)
                        e.dma_start(BIAS[:, 1 - par, :, :], ali_a[P + 1]).then_inc(S[f"bias_full{1 - par}"], 16)
                        raw(w + 6)
                        raw(w + 7)
                for P in range(4, 8):
                    body(P, P % 2, "B", "B" if P < 7 else None, True)
            else:
                iterations(e, body, lambda *a: None, 1)

        def out_projection(o):
            last = 8 * o + 7
            kind = "BC"[o]
            e.wait_ge(S["fill_done"], 48 * (o + 1))
            e.wait_ge(S["y_out0"], 1 + 16 * (28 if o == 0 else 46))
            e.wait_ge(S["y_out1"], 1 + 16 * (28 if o == 0 else 46))
            for k in range(KC - 1):
                e.dma_start(Y[:, k, :], y_dram[k]).then_inc(S[f"yl_full{k}"], 16)
            e.wait_ge(S["y_out0"], 1 + 16 * (32 if o == 0 else 48))
            e.wait_ge(S["y_out1"], 1 + 16 * (32 if o == 0 else 48))
            e.dma_start(Y[:, KC - 1, :], y_dram[KC - 1]).then_inc(S[f"yl_full{KC - 1}"], 16)
            load_x(x_in if o == 0 else x_dram)
            with e.Fori(0, KC // 2) as i:
                for b in range(2):
                    raw(W_OUT[o] + 2 * i + b + 2)

        def ffn(n):
            e.wait_ge(S["op_done"], 1 + 16 * (n + 1))

            def body(t, last=False):
                w = W_FFN[n] + 2 * t
                e.wait_ge(S["d_lo"], 1 + FT * n + t)
                e.dma_start(DR[:, :], wdown[FT * n + t]).then_inc(S["d_full"], 16)
                if not last:
                    raw(w + 2)
                    raw(w + 3)

            with e.Fori(0, FT - 1) as t:
                body(t)
            body(FT - 1, last=n == 1)

        e.dma_start(GAIN[:, :, :], gains).then_inc(S["gains_full"], 16)
        e.dma_start(LV[:, :, :], lams.partition_broadcast(128)).then_inc(S["gains_full"], 16)
        e.dma_start(SUBG[:, 0:1], subln).then_inc(S["gains_full"], 16)
        for c in range(2):
            e.dma_start(X[:, 2 * c:2 * c + 2, :], x_in[:, 2 * c:2 * c + 2, :]).then_inc(S[f"x_full{c}"], 16)
        for x in range(2):
            e.dma_start(WR[:, x, :], wstrips[0, x]).then_inc(S[f"raw_full{x}"], 16)
        for c in range(2, 4):
            e.dma_start(X[:, 2 * c:2 * c + 2, :], x_in[:, 2 * c:2 * c + 2, :]).then_inc(S[f"x_full{c}"], 16)
        raw(1)
        attention(0)
        out_projection(0)
        ffn(0)
        for j in range(KC):
            e.wait_ge(S["d_free"], 4 + 16 * (FT - 1) + 2 * j + 2)
            e.dma_start(x_dram[:, j, :], X[:, j, :]).then_inc(S["x_saved"], 16)
        e.wait_ge(S["x_saved"], 16 * KC)
        attention(1)
        out_projection(1)
        ffn(1)
        for k in range(KC):
            e.wait_ge(S["out_ready"], k + 1)
            e.dma_start(out[:, k, :], X[:, k, :]).then_inc(S["out_full"], 16)
        e.wait_ge(S["out_full"], 16 * KC)

    def pool_program(e):
        e.memset(ONES[:, :], 1.0).then_inc(S["ones_ready"], 1)
        e.memset(IDENT[:, :], 0.0).then_inc(S["ident_ready"], 1)
        e.memset(EPS[:, 0:1], RMS_EPS).then_inc(S["ones_ready"], 1)
        e.memset(EPS[:, 1:2], SUBLN_EPS).then_inc(S["ones_ready"], 1)
        e.wait_ge(S["ident_ready"], 1)
        e.affine_select(out=IDENT[:, :], in_=IDENT[:, :], compare_op=ALU.not_equal, fill=1.0, base=0,
                        pattern=[[-1, 128]], channel_multiplier=1).then_inc(S["ident_ready"], 1)

        def norm1(P, n, kind):
            k0, nk = key_tiles(kind, n)
            e.wait_ge(S["rec_done"], 16 * P + 2 * n + 2)
            e.sem_inc(S["pool_passed"], 1)
            e.tensor_scalar(E1[:, n % 2, 0:128 * nk], E1[:, n % 2, 0:128 * nk], ST[:, n % 2, 5:6], None,
                            ALU.mult).then_inc(S["p1_ready"], 1)

        def head(P, par, kind):
            norm1(P, 0, kind)

        def body(P, par, kind, nxt, looks):
            for n in range(NQ):
                if n < NQ - 1:
                    norm1(P, n + 1, kind)
                elif looks:
                    norm1(P + 1, 0, kind)

        def add_squares(N):
            if N:
                e.wait_ge(S["ssq_done"], N)
            e.memset(ACC[:, :], 0.0).then_inc(S["acc_zero"], 1)
            e.wait_ge(S["acc_zero"], N // 2 + 1)
            for j in range(KC):
                e.wait_ge(S["sq_done"], 8 * N + j + 1)
                if 8 * N + j:
                    e.wait_ge(S["sadd"], 8 * N + j)
                e.tensor_tensor(ACC[:, :], ACC[:, :], SQ[:, j % 2, :], ALU.add).then_inc(S["sadd"], 1)

        add_squares(0)
        iterations(e, body, head, 0)
        add_squares(2)
        add_squares(4)

    def act_program(e):
        def w_split(w, slot, used=None):
            if used:
                e.wait_ge(S[used[0]], used[1])
            for x in range(2):
                e.wait_ge(S[f"raw_full{x}"], 16 * w + 16)
                e.activation(WS[:, slot, 0, 512 * x:512 * x + 512], WR[:, x, :], ACT.Copy).then_inc(S["w_hi"], 1)

        def prep_chunk(N, j, b):
            if not (isinstance(j, int) and 8 * N + j < 1):
                e.wait_ge(S["sadd"], 8 * N + j - 1)
            e.activation(SQ[:, b, :], X[:, j, :], ACT.Square).then_inc(S["sq_done"], 1)
            if N < 4:
                e.activation((FH if N % 2 else HH)[:, j, :], X[:, j, :], ACT.Copy,
                             scale=GAIN[:, N, bass.ds(j, 1)]).then_inc(S["xhi_done"], 1)

        def root(N):
            e.wait_ge(S["ssq_done"], N + 1)
            e.activation(RT[:, 0, :], PS[:, SSQ_BANK, 0:NQ], ACT.Sqrt, scale=1.0 / D,
                         bias=EPS[:, 0:1]).then_inc(S["sqrt_done"], 1)

        def rstd(N):
            e.wait_ge(S["spread_done"], N + 1)
            e.activation(RSTD[:, :], banks(SSQ_BANK, 2), ACT.Copy).then_inc(S["rstd_done"], 1)

        def xy(P, par, n):
            e.wait_ge(S["fill_evac"], 6 * P + (5 if n < 4 else 6))
            e.wait_ge(S["qk_done"], 1 + 16 * P + 2 * n)
            q = QR[:, par, 128 * n:128 * n + 128]
            e.activation(XY[0:64, 0, :], q[0:64], ACT.Copy).then_inc(S["xy_act"], 1)
            e.activation(XY[64:128, 1, :], q[64:128], ACT.Copy).then_inc(S["xy_act"], 1)

        def exp(P, n, m, kind):
            k0, nk = key_tiles(kind, n)
            e.wait_ge(S["ttr_done"], 1 + 16 * P + 2 * n + m + 1)
            t = e_tile(kind, n, m, 128 * nk)
            e.activation(t, t, ACT.Exp, scale=-1.0, bias=ST[:, n % 2, m:m + 1],
                         accum_out=ST[:, n % 2, 2 + m:3 + m]).then_inc(S["exp_done"], 1)

        def escale(P, n):
            e.wait_ge(S["c1_ready"], 8 * P + n + 1 - 64)
            e.activation(E1[:, n % 2, :], E1[:, n % 2, :], ACT.Copy, scale=ST[:, n % 2, 6:7]).then_inc(S["escaled"], 1)

        def khi(P, par, kk, layer, bank=FILL_BANK):
            e.wait_ge(S["kmul_done"], 2 * P + kk + 1)
            c = 512 * kk
            full = k_full(layer, bank)
            e.activation(KS[0:64, par, 0, c:c + 512], full[0:64], ACT.Copy).then_inc(S["khi_done"], 1)
            e.activation(KS[64:128, par, 1, c:c + 512], full[64:128], ACT.Copy).then_inc(S["khi_done"], 1)

        def vhi(P, par, vv, kind):
            e.wait_ge(S["tv_done"], 2 * P + vv + 1)
            if kind == "C":
                dst = VS[:, par, 4 * vv:4 * vv + 4, 0:128]
                src = PS[:, PV_BANK, :].rearrange("p (k d) -> p k d", k=4)
            else:
                dst = VS[:, par, 4 * vv:4 * vv + 4, :].rearrange("p k (m s d) -> p k m s d", m=2, s=2)[:, :, :, 0, :]
                src = PS[:, PV_BANK, :].rearrange("p (k m d) -> p k m d", k=4, m=2)
            e.activation(dst, src, ACT.Copy).then_inc(S["vhi_done"], 1)

        def hi(P, n, m, kind):
            k0, nk = key_tiles(kind, n)
            b = m if kind != "C" else (n // 2) % 2
            e.wait_ge(S["t_done"], t_count(P, n, m, kind))
            e.wait_ge(S["pv_done"], unit(P, n, m, kind) + 1)
            c = 128 * (n % 2)
            e.activation(AT[:, b, k0:k0 + nk, 0, c:c + 128],
                         banks(T_BANK, 2)[:, 0:128 * nk].rearrange("p (k q) -> p k q", k=nk),
                         ACT.Copy).then_inc(S["hi_done"], 1)

        def y_copy(P, n, m, kind):
            u = unit(P, n, m, kind)
            e.wait_ge(S["pv_done"], u + 3)
            e.wait_ge(S[f"y_out{m}"], 1 + 64 * P + 16 * (n // 2))
            e.activation(YS[0:64, m, :], PS[64:128, PV_BANK, 0:256], ACT.Copy).then_inc(S["y_copy"], 1)

        def y_dma(P, n, m, kind):
            e.wait_ge(S["y_done"], 1 + unit(P, n, m, kind) + 1)
            c = 256 * (n // 2)
            if kind == "C":
                b = (n // 2) % 2
                e.dma_start(y_dram[P - 8, :, c:c + 256], YS[:, b, :]).then_inc(S[f"y_out{b}"], 16)
            else:
                e.dma_start(y_dram[P, 64 * m:64 * m + 64, c:c + 256], YS[0:64, m, :]).then_inc(S[f"y_out{m}"], 16)

        def y_square(k):
            e.wait_ge(S[f"yl_full{k}"], 32)
            e.activation(YQ[:, k, :], Y[:, k, :], ACT.Square).then_inc(S["ysq_done"], 1)

        def y_root(a, b):
            e.wait_ge(S["yssq_done"], b)
            e.activation(RT[:, a:b, :].rearrange("p k t -> p (k t)"), PS[:, FILL_BANK, NQ * a:NQ * b], ACT.Sqrt,
                         scale=1.0 / 128, bias=EPS[:, 1:2]).then_inc(S["ysqrt_done"], 1)

        def y_high(o, k):
            if o == 0:
                e.wait_ge(S[f"yl_full{k}"], 16)
            else:
                e.wait_ge(S["ynorm_done"], k + 1)
            e.activation(HH[:, k, :], Y[:, k, :], ACT.Copy).then_inc(S["yhi_done"], 1)

        def attention(layer):
            P0, kind = 8 * layer, "AC"[layer]
            w0 = strip_of(P0, layer)
            w_split(w0 + 1, 1, ("u_done", FT * layer) if layer else None)
            root(2 * layer)
            rstd(2 * layer)
            w_split(w0 + 2, 0, ("fill_done", 6 * P0 + 2))
            vhi(P0, 0, 0, kind)
            khi(P0, 0, 0, layer, FIRST_BANKS[2])
            vhi(P0, 0, 1, kind)
            khi(P0, 0, 1, layer, FIRST_BANKS[3])
            w_split(w0 + 3, 1, ("fill_done", 6 * P0 + 4))

            def start(P, par, kind):
                xy(P, par, 0)
                exp(P, 0, 0, kind)
                xy(P, par, 1)
                exp(P, 0, 1, kind)
                if kind == "C":
                    escale(P, 0)

            def body(P, par, kind, nxt, looks):
                w = strip_of(P, layer)
                for n in range(NQ):
                    go = n < NQ - 1 or looks
                    Pn, nn = (P, n + 1) if n < NQ - 1 else (P + 1, 0)
                    if nxt and kind != "C" and EVAC_START[kind].get(n) in (2, 3):
                        khi(P + 1, 1 - par, EVAC_START[kind][n] - 2, layer)
                    if kind != "C" or n == NQ - 1:
                        hi(P, n, 0, kind)
                    if go:
                        exp(Pn, nn, 0, kind)
                    if kind == "C" and go:
                        exp(Pn, nn, 1, kind)
                    if n < NQ - 2:
                        xy(P, par, n + 2)
                    elif looks:
                        xy(P + 1, 1 - par, n - 6)
                    if kind == "C":
                        if n < NQ - 1:
                            hi(P, n, 0, kind)
                        if go:
                            escale(Pn, nn)
                        for halves in (EVAC_START, EVAC_MID):
                            if nxt and halves[kind].get(n) in (2, 3):
                                khi(P + 1, 1 - par, halves[kind][n] - 2, layer)
                    else:
                        hi(P, n, 1, kind)
                        if go:
                            exp(Pn, nn, 1, kind)
                    if nxt and n in TV_AT[kind]:
                        vhi(P + 1, 1 - par, TV_AT[kind][n], kind)
                    if n % 2 and kind != "C":
                        y_copy(P, n, 0, kind)
                    if nxt and n in SPLIT_AT:
                        w_split(w + SPLIT_AT[n], (par + SPLIT_AT[n]) % 2, ("fill_done", 6 * P + SPLIT_USED[n]))
                    if n % 2 and kind != "C":
                        y_copy(P, n, 1, kind)
                        y_dma(P, n, 0, kind)
                        y_dma(P, n, 1, kind)
                    if kind == "C" and n in (2, 4, 6):
                        y_dma(P, n - 1, 0, kind)
                    if nxt is None and n < NQ - 1:
                        if layer:
                            y_square(n)
                        else:
                            y_high(0, n)
                if kind == "C":
                    y_dma(P, NQ - 1, 0, kind)

            iterations(e, body, start, layer)

        def out_projection(o):
            if o == 0:
                y_high(0, KC - 1)
            else:
                y_root(0, KC - 1)
                for k in range(5):
                    y_high(1, k)
                y_square(KC - 1)
                y_high(1, 5)
                y_root(KC - 1, KC)
                y_high(1, 6)
                y_high(1, 7)
            N = 2 * o + 1
            e.wait_ge(S["fill_done"], 48 * (o + 1))
            with e.Fori(0, KC // 2) as i:
                for b in range(2):
                    j = 2 * i + b
                    w_split(W_OUT[o] + j + 1, (b + 1) % 2, ("op_done", 1 + 16 * o + 2 * j))
                    e.wait_ge(S["op_free"], 16 * o + 2 * j + 2 + 4)
                    prep_chunk(N, j, b)
            root(N)

        def ffn(n):
            def body(t, first=False, last=False, final=False):
                TT = FT * n + t
                if not first:
                    e.wait_ge(S["d_full"], 16 * TT)
                    e.wait_ge(S["d_done"], 1 + 16 * (TT - 1))
                    e.activation(DS[:, 0, :], DR[:, :], ACT.Copy).then_inc(S["d_hi"], 1)
                    e.wait_ge(S["prod_done"], TT)
                    e.activation(AH[:, :], PROD[:, :], ACT.Copy).then_inc(S["ahi_done"], 1)
                if not last:
                    w_split(W_FFN[n] + 2 * t + 1, 1, ("op_done", 1 + 16 * (n + 1)) if first else ("u_done", TT))
                    if first:
                        rstd(2 * n + 1)
                    e.wait_ge(S["gmul_done"], TT + 1)
                    e.activation(SIL[:, :], banks(G_BANK, 2), ACT.Silu).then_inc(S["sil_done"], 1)
                    if not final:
                        w_split(W_FFN[n] + 2 * t + 2, 0, ("g_done", TT + 1))

            body(0, first=True)
            with e.Fori(1, FT - 1) as t:
                body(t)
            body(FT - 1, final=n == 1)
            body(FT, last=True)
            N = 2 * n + 2
            for j in range(KC):
                e.wait_ge(S["d_free"], 4 + 16 * (FT * (n + 1) - 1) + 2 * j + 2)
                prep_chunk(N, j, j % 2)
            if n == 1:
                root(N)

        w_split(0, 0)
        for name in ("y_out0", "y_out1"):
            e.sem_inc(S[name], 1)
        e.wait_ge(S["lam_ready"], 2)
        e.activation(NEGLAM[:, 0:2], NEGLAM[:, 2:4], ACT.Exp).then_inc(S["lam_ready"], 1)
        e.wait_ge(S["gains_full"], 48)
        e.wait_ge(S["ones_ready"], 3)
        for j in range(KC):
            e.wait_ge(S[f"x_full{j // 2}"], 16)
            prep_chunk(0, j, j % 2)
        attention(0)
        out_projection(0)
        ffn(0)
        attention(1)
        out_projection(1)
        ffn(1)
        rstd(4)

    def dve_program(e):
        def w_split(w, slot):
            for x in range(2):
                e.wait_ge(S["w_hi"], 2 * w + x + 1)
                c = 512 * x
                e.tensor_tensor(WS[:, slot, 1, c:c + 512], WR[:, x, :], f(WS[:, slot, 0, c:c + 512]),
                                ALU.subtract).then_inc(S["w_lo"], 1)

        def zero_acc(N):
            e.wait_ge(S["ssq_done"], N)
            e.memset(ACC[:, :], 0.0).then_inc(S["acc_zeroed"], 1)

        def prep_chunk(N, j, b):
            if N % 2:
                e.wait_ge(S["sq_done"], 8 * N + j + 1)
                e.wait_ge(S["acc_zeroed"], N // 2 + 1)
                e.wait_ge(S["sadd"], 8 * N + j)
                e.tensor_tensor(ACC[:, :], ACC[:, :], SQ[:, b, :], ALU.add).then_inc(S["sadd"], 1)
            if N < 4:
                e.wait_ge(S["xhi_done"], 8 * N + j + 1)
                high, low = (FH, FL) if N % 2 else (HH, HL)
                e.scalar_tensor_tensor(out=low[:, j, :], in0=X[:, j, :], scalar=GAIN[:, N, bass.ds(j, 1)],
                                       in1=f(high[:, j, :]), op0=ALU.mult, op1=ALU.subtract).then_inc(S["xlo_done"], 1)

        def root(N):
            e.wait_ge(S["sqrt_done"], N + 1)
            e.reciprocal(RT[:, 0, :], RT[:, 0, :]).then_inc(S["rinv_done"], 1)

        def evac(P, par, k, layer, bank=FILL_BANK, later=False):
            e.wait_ge(S["fill_done"], 6 * P + k + 1)
            half = k % 2
            c = 512 * half
            ps = PS[:, bank, :]
            r = RSTD[:, c:c + 512]
            if k < 2:
                e.tensor_tensor(QR[:, par, c:c + 512], ps, r, ALU.mult).then_inc(S["fill_evac"], 1)
            elif k >= 4:
                e.wait_ge(S["tv_done"], 2 * P + 2)
                e.scalar_tensor_tensor(out=QR[:, par, c:c + 512], in0=ps, scalar=-DH ** -0.5, in1=r,
                                       op0=ALU.mult, op1=ALU.mult).then_inc(S["fill_evac"], 1)
            else:
                full = k_full(layer, bank)
                if layer:
                    e.wait_ge(S["fill_evac"], 6 * P + k)
                e.tensor_tensor(full, ps, r, ALU.mult).then_inc(S["kmul_done"], 1)
                if not later:
                    klo(P, par, k, layer, bank)

        def klo(P, par, k, layer, bank=FILL_BANK):
            half = k % 2
            c = 512 * half
            full = k_full(layer, bank)
            e.wait_ge(S["khi_done"], 4 * P + 2 * half + 2)
            e.tensor_tensor(KS[64:128, par, 0, c:c + 512], full[0:64], f(KS[0:64, par, 0, c:c + 512]), ALU.subtract)
            e.tensor_tensor(KS[0:64, par, 1, c:c + 512], full[64:128], f(KS[64:128, par, 1, c:c + 512]),
                            ALU.subtract).then_inc(S["fill_evac"], 1)

        def vlo(P, par, vv, kind):
            e.wait_ge(S["vhi_done"], 2 * P + vv + 1)
            if kind == "C":
                v = VS[:, par, 4 * vv:4 * vv + 4, :]
                dst, high = v[:, :, 128:256], v[:, :, 0:128]
                src = PS[:, PV_BANK, :].rearrange("p (k d) -> p k d", k=4)
            else:
                v = VS[:, par, 4 * vv:4 * vv + 4, :].rearrange("p k (m s d) -> p k m s d", m=2, s=2)
                dst, high = v[:, :, :, 1, :], v[:, :, :, 0, :]
                src = PS[:, PV_BANK, :].rearrange("p (k m d) -> p k m d", k=4, m=2)
            e.tensor_tensor(dst, src, f(high), ALU.subtract).then_inc(S["vlo_done"], 1)

        def xy_cross(P, par, n):
            e.wait_ge(S["fill_evac"], 6 * P + (5 if n < 4 else 6))
            e.wait_ge(S["qk_done"], 1 + 16 * P + 2 * n)
            q = QR[:, par, 128 * n:128 * n + 128]
            e.tensor_copy(XY[64:128, 0, :], q[0:64])
            e.tensor_copy(XY[0:64, 1, :], q[64:128])

        def xy_low(P, par, n):
            q = QR[:, par, 128 * n:128 * n + 128]
            e.wait_ge(S["xy_act"], 16 * P + 2 * n + 2)
            e.tensor_tensor(XY[0:64, 2, :], q[0:64], f(XY[0:64, 0, :]), ALU.subtract)
            e.tensor_tensor(XY[64:128, 3, :], q[64:128], f(XY[64:128, 1, :]), ALU.subtract).then_inc(S["xy_dve"], 1)

        def ttr(P, par, n, m, kind):
            k0, nk = key_tiles(kind, n)
            e.wait_ge(S["qk_done"], 1 + 16 * P + 2 * n + m + 1)
            c = bias_start(kind, n)
            t = e_tile(kind, n, m, 128 * nk)
            e.sem_inc(S["dve_passed"], 1)
            e.tensor_tensor_reduce(out=t, in0=banks(S_BANK[m], 2)[:, 0:128 * nk],
                                   in1=BIAS[:, par, m if kind != "C" else 0, c:c + 128 * nk],
                                   scale=1.0, scalar=3e38, op0=ALU.add, op1=ALU.min,
                                   accum_out=ST[:, n % 2, m:m + 1]).then_inc(S["ttr_done"], 1)

        def recip(P, n, m):
            e.wait_ge(S["exp_done"], 16 * P + 2 * n + m + 1)
            e.reciprocal(ST[:, n % 2, 4 + m:5 + m], ST[:, n % 2, 2 + m:3 + m]).then_inc(S["rec_done"], 1)

        def norm0(P, n, kind):
            k0, nk = key_tiles(kind, n)
            e.wait_ge(S["rec_done"], 16 * P + 2 * n + 1)
            e.tensor_scalar(E0[:, 0:128 * nk], E0[:, 0:128 * nk], ST[:, n % 2, 4:5], None,
                            ALU.mult).then_inc(S["p0_ready"], 1)

        def factors(P, n):
            e.wait_ge(S["exp_done"], 16 * P + 2 * n + 2)
            e.reciprocal(ST[:, n % 2, 4:6], ST[:, n % 2, 2:4]).then_inc(S["rec_done"], 1)
            e.wait_ge(S["rec_done"], 128 + 8 * P + n + 1 - 64)
            e.tensor_tensor(ST[:, n % 2, 6:7], ST[:, n % 2, 5:6], NEGLAM[:, 2:3], ALU.mult).then_inc(S["c1_ready"], 1)

        def combine(P, n):
            e.wait_ge(S["escaled"], 8 * P + n + 1 - 64)
            t = e_tile("C", n, 0)
            e.scalar_tensor_tensor(out=t, in0=t, scalar=ST[:, n % 2, 4:5], in1=E1[:, n % 2, :],
                                   op0=ALU.mult, op1=ALU.add).then_inc(S["p0_ready"], 1)

        def lo(P, n, m, kind):
            k0, nk = key_tiles(kind, n)
            b = m if kind != "C" else (n // 2) % 2
            e.wait_ge(S["hi_done"], t_count(P, n, m, kind))
            c = 128 * (n % 2)
            e.tensor_tensor(AT[:, b, k0:k0 + nk, 1, c:c + 128],
                            banks(T_BANK, 2)[:, 0:128 * nk].rearrange("p (k q) -> p k q", k=nk),
                            f(AT[:, b, k0:k0 + nk, 0, c:c + 128]), ALU.subtract).then_inc(S["lo_done"], 1)

        def y_add(P, n, m, kind):
            if kind == "C":
                b = (n // 2) % 2
                e.wait_ge(S["pv_done"], unit(P, n, m, kind) + 3)
                e.wait_ge(S[f"y_out{b}"], 1 + 16 * (32 + 2 * (P - 8) + n // 4))
                e.tensor_copy(YS[:, b, :], PS[:, PV_BANK, 0:256]).then_inc(S["y_done"], 1)
            else:
                e.wait_ge(S["y_copy"], unit(P, n, m, kind) + 1)
                e.tensor_tensor(YS[0:64, m, :], PS[0:64, PV_BANK, 0:256], YS[0:64, m, :],
                                ALU.add).then_inc(S["y_done"], 1)

        def bias_ready(P, par, kind):
            e.wait_ge(S[f"bias_full{par}"], 8 * P - 8 * par + 16)

        def negate(P, par):
            bias_ready(P, par, "B")
            for m in range(2):
                e.tensor_scalar(BIAS[:, par, m, 0:TAB_B], BIAS[:, par, m, 0:TAB_B], -1.0, None,
                                ALU.mult).then_inc(S["bneg_done"], 1)

        def attention(layer):
            P0, kind = 8 * layer, "AC"[layer]
            w0 = strip_of(P0, layer)
            w_split(w0 + 1, 1)
            root(2 * layer)
            if layer:
                e.wait_ge(S["x_saved"], 16 * KC)
            e.memset(f(XY[:, 2:4, :]), 0.0).then_inc(S["xy_zero"], 1)
            e.wait_ge(S["xy_zero"], layer + 1)
            e.wait_ge(S["rstd_done"], 2 * layer + 1)
            evac(P0, 0, 0, layer, FIRST_BANKS[0])
            w_split(w0 + 2, 0)
            evac(P0, 0, 1, layer, FIRST_BANKS[1])
            vlo(P0, 0, 0, kind)
            evac(P0, 0, 2, layer, FIRST_BANKS[2])
            vlo(P0, 0, 1, kind)
            evac(P0, 0, 3, layer, FIRST_BANKS[3])
            evac(P0, 0, 4, layer, FIRST_BANKS[4])
            w_split(w0 + 3, 1)
            evac(P0, 0, 5, layer, FIRST_BANKS[5])

            def start(P, par, kind):
                bias_ready(P, par, kind)
                if kind == "B":
                    negate(P, par)
                    e.wait_ge(S["bneg_done"], 2 * (P - 4) + 2)
                xy_cross(P, par, 0)
                xy_low(P, par, 0)
                ttr(P, par, 0, 0, kind)
                ttr(P, par, 0, 1, kind)
                xy_cross(P, par, 1)
                xy_low(P, par, 1)
                if kind == "C":
                    factors(P, 0)
                    combine(P, 0)
                else:
                    recip(P, 0, 0)
                    norm0(P, 0, kind)
                    recip(P, 0, 1)

            def body(P, par, kind, nxt, looks):
                w = strip_of(P, layer)
                for n in range(NQ):
                    go = n < NQ - 1 or looks
                    Pn, nn, parn = (P, n + 1, par) if n < NQ - 1 else (P + 1, 0, 1 - par)
                    if nxt and kind != "C" and n in EVAC_START[kind]:
                        evac(P + 1, 1 - par, EVAC_START[kind][n], layer)
                    if go:
                        if n == NQ - 1:
                            bias_ready(P + 1, 1 - par, kind)
                            if kind == "B":
                                e.wait_ge(S["bneg_done"], 2 * (P + 1 - 4) + 2)
                        ttr(Pn, parn, nn, 0, kind)
                    if kind == "C" and n == NQ - 1:
                        lo(P, n, 0, kind)
                    if kind == "C" and go:
                        ttr(Pn, parn, nn, 1, kind)
                    if kind != "C":
                        lo(P, n, 0, kind)
                        if go:
                            recip(Pn, nn, 0)
                            norm0(Pn, nn, kind)
                            ttr(Pn, parn, nn, 1, kind)
                    if nxt and n in EVAC_MID[kind]:
                        evac(P + 1, 1 - par, EVAC_MID[kind][n], layer, later=kind == "C")
                    if n < NQ - 2:
                        xy_item = (P, par, n + 2)
                    elif looks:
                        xy_item = (P + 1, 1 - par, n - 6)
                    else:
                        xy_item = None
                    if xy_item:
                        xy_cross(*xy_item)
                    if kind == "C" and go:
                        factors(Pn, nn)
                    if xy_item:
                        xy_low(*xy_item)
                    if kind == "C":
                        if nxt and n + 1 in EVAC_START[kind]:
                            evac(P + 1, 1 - par, EVAC_START[kind][n + 1], layer, later=True)
                        if n < NQ - 1:
                            lo(P, n, 0, kind)
                        if go:
                            combine(Pn, nn)
                        for halves in (EVAC_START, EVAC_MID):
                            if nxt and halves[kind].get(n) in (2, 3):
                                klo(P + 1, 1 - par, halves[kind][n], layer)
                    else:
                        lo(P, n, 1, kind)
                        if go:
                            recip(Pn, nn, 1)
                    if nxt and n in TV_AT[kind]:
                        vlo(P + 1, 1 - par, TV_AT[kind][n], kind)
                    if nxt == "B" and n == 3:
                        negate(P + 1, 1 - par)
                    if n % 2 and kind != "C":
                        y_add(P, n, 0, kind)
                    if kind == "C" and n in (2, 4, 6):
                        y_add(P, n - 1, 0, kind)
                    if nxt and n in SPLIT_AT:
                        w_split(w + SPLIT_AT[n], (par + SPLIT_AT[n]) % 2)
                    if n % 2 and kind != "C":
                        y_add(P, n, 1, kind)
                    if nxt is None and n < NQ - 1 and layer == 0:
                        y_low(0, n)
                if nxt:
                    evac(P + 1, 1 - par, 5, layer)
                if kind == "C":
                    y_add(P, NQ - 1, 0, kind)

            iterations(e, body, start, layer)

        def y_low(o, k):
            e.wait_ge(S["yhi_done"], 8 * o + k + 1)
            e.tensor_tensor(HL[:, k, :], Y[:, k, :], f(HH[:, k, :]), ALU.subtract).then_inc(S["ylo_done"], 1)

        def out_projection(o):
            if o == 0:
                y_low(0, KC - 1)
            else:
                for k in range(KC + 1):
                    if k in (0, KC - 1):
                        rt = RT[:, k:(KC - 1 if k == 0 else KC), :].rearrange("p k t -> p (k t)")
                        e.wait_ge(S["ysqrt_done"], 1 if k == 0 else 2)
                        e.reciprocal(rt, rt).then_inc(S["yrec_done"], 1)
                    if k < KC:
                        e.wait_ge(S["yspread_done"], k + 1)
                        e.scalar_tensor_tensor(out=Y[:, k, :], in0=Y[:, k, :], scalar=SUBG[:, 1:2],
                                               in1=banks(2 * (k % 2), 2), op0=ALU.mult,
                                               op1=ALU.mult).then_inc(S["ynorm_done"], 1)
                    if k:
                        y_low(1, k - 1)
            N = 2 * o + 1
            zero_acc(N)
            for c in range(4):
                e.wait_ge(S[f"x_full{c}"], 16 * (o + 2))
            with e.Fori(0, KC // 2) as i:
                for b in range(2):
                    j = 2 * i + b
                    w_split(W_OUT[o] + j + 1, (b + 1) % 2)
                    for h in range(2):
                        e.wait_ge(S["op_done"], 1 + 16 * o + 2 * j + h + 1)
                        xs = X[:, j, 512 * h:512 * h + 512]
                        e.tensor_tensor(xs, PS[:, 2 * b + h, :], xs, ALU.add).then_inc(S["op_free"], 1)
                    prep_chunk(N, j, b)
            root(N)

        def ffn(n):
            def body(t, first=False, last=False, final=False):
                TT = FT * n + t
                if not first:
                    e.wait_ge(S["u_done"], TT)
                    e.tensor_tensor(UT[:, :], banks(U_BANK, 2), RSTD[:, :], ALU.mult).then_inc(S["umul_done"], 1)
                    e.wait_ge(S["sil_done"], TT)
                    e.wait_ge(S["umul_done"], TT)
                    e.tensor_tensor(PROD[:, :], SIL[:, :], UT[:, :], ALU.mult).then_inc(S["prod_done"], 1)
                    e.wait_ge(S["d_hi"], TT)
                    e.tensor_tensor(DS[:, 1, :], DR[:, :], f(DS[:, 0, :]), ALU.subtract).then_inc(S["d_lo"], 1)
                    e.wait_ge(S["ahi_done"], TT)
                    e.tensor_tensor(AL[:, :], PROD[:, :], f(AH[:, :]), ALU.subtract).then_inc(S["alo_done"], 1)
                if not last:
                    w_split(W_FFN[n] + 2 * t + 1, 1)
                for ev in range(16):
                    if last and ev % 2 == 0 and ev >= 4:
                        prep_chunk(2 * n + 2, ev // 2 - 2, ev // 2 % 2)
                    if not first:
                        e.wait_ge(S["d_done"], 1 + 16 * (TT - 1) + ev + 1)
                        xs = X[:, ev // 2, 512 * (ev % 2):512 * (ev % 2) + 512]
                        e.tensor_tensor(xs, PS[:, D_BANK + ev % 4, :], xs, ALU.add).then_inc(S["d_free"], 1)
                    if ev == 5 and not last:
                        e.wait_ge(S["g_done"], TT + 1)
                        if first:
                            e.wait_ge(S["rstd_done"], 2 * n + 2)
                        g = banks(G_BANK, 2)
                        e.tensor_tensor(g, g, RSTD[:, :], ALU.mult).then_inc(S["gmul_done"], 1)
                    if ev == 8 and not last and not final:
                        w_split(W_FFN[n] + 2 * t + 2, 0)

            body(0, first=True)
            with e.Fori(1, FT - 1) as t:
                body(t)
            body(FT - 1, final=n == 1)
            body(FT, last=True)
            N = 2 * n + 2
            for j in range(KC - 2, KC):
                prep_chunk(N, j, j % 2)
            if n == 1:
                root(N)

        w_split(0, 0)
        e.wait_ge(S["gains_full"], 48)
        e.tensor_tensor(LP[:, 0, :], LV[:, 0, :], LV[:, 1, :], ALU.mult).then_inc(S["consts_ready"], 1)
        e.tensor_tensor(LP[:, 1, :], LV[:, 2, :], LV[:, 3, :], ALU.mult).then_inc(S["consts_ready"], 1)
        e.wait_ge(S["consts_ready"], 2)
        e.reduce_sum(NEGLAM[:, 2:3], LP[:, 0, :], axis=mybir.AxisListType.X).then_inc(S["lam_ready"], 1)
        e.reduce_sum(NEGLAM[:, 3:4], LP[:, 1, :], axis=mybir.AxisListType.X).then_inc(S["lam_ready"], 1)
        e.tensor_scalar(SUBG[:, 1:2], SUBG[:, 0:1], 1.0 - LAM_INIT, None, ALU.mult).then_inc(S["consts_ready"], 1)
        e.wait_ge(S["lam_ready"], 3)
        e.tensor_tensor(NEGLAM[:, 3:4], NEGLAM[:, 1:2], NEGLAM[:, 0:1], ALU.subtract).then_inc(S["consts_ready"], 1)
        e.wait_ge(S["consts_ready"], 4)
        e.tensor_scalar(NEGLAM[:, 2:3], NEGLAM[:, 3:4], -LAM_INIT, None, ALU.add).then_inc(S["consts_ready"], 1)
        for name in ("ttr_done", "y_done", "lo_done", "d_lo"):
            e.sem_inc(S[name], 1)
        e.sem_inc(S["op_free"], 4)
        e.sem_inc(S["d_free"], 4)
        for j in range(KC):
            prep_chunk(0, j, j % 2)
        attention(0)
        out_projection(0)
        ffn(0)
        attention(1)
        out_projection(1)
        ffn(1)
        e.wait_ge(S["rstd_done"], 5)
        for k in range(KC):
            e.scalar_tensor_tensor(out=X[:, k, :], in0=X[:, k, :], scalar=GAIN[:, 4, k:k + 1], in1=RSTD[:, :],
                                   op0=ALU.mult, op1=ALU.mult).then_inc(S["out_ready"], 1)

    def pe_program(e):
        def three(ps, wh, wl, xh, xl, start, stop):
            e.matmul(ps, wh, xh, start=start, stop=False)
            e.matmul(ps, wh, xl, start=False, stop=False)
            return e.matmul(ps, wl, xh, start=False, stop=stop)

        def sums(src, bank, done, at=0):
            for t in range(NQ):
                last = e.matmul(PS[:, bank, at + t:at + t + 1], src[:, 128 * t:128 * t + 128], ONES[:, 0:1],
                                start=True, stop=True)
            last.then_inc(S[done], 1)

        def spread(col, bank, done):
            for t in range(NQ):
                last = e.matmul(PS[:, bank + t // 4, 128 * (t % 4):128 * (t % 4) + 128],
                                col[:, t:t + 1].to_broadcast([128, 128]), IDENT[:, :], start=True, stop=True)
            last.then_inc(S[done], 1)

        def ssq(N):
            e.wait_ge(S["sadd"], 8 * N + 8)
            e.wait_ge(S["ones_ready"], 1)
            sums(ACC, SSQ_BANK, "ssq_done")

        def spread_rstd(N):
            e.wait_ge(S["rinv_done"], N + 1)
            spread(RT[:, 0, :], SSQ_BANK, "spread_done")

        def y_sums(k):
            e.wait_ge(S["ysq_done"], k + 1)
            sums(YQ[:, k, :], FILL_BANK, "yssq_done", at=NQ * k)

        def fill(P, par, k, a, b, layer, prep=None, bank=None):
            w = strip_of(P, layer) + k // 2
            h = k % 2
            slot = (par + k // 2) % 2
            if a == 0 and bank is None:
                if layer and k in (3, 4):
                    e.wait_ge(S["kmul_done"], 2 * P + k - 2)
                else:
                    e.wait_ge(S["fill_evac"], 6 * P + k)
            ps = PS[:, FILL_BANK if bank is None else bank, :]
            for g in range(a, b):
                c, part = g // 3, g % 3
                if h == 0 and g in (0, 12):
                    e.wait_ge(S["w_lo"], 2 * w + 1 + g // 12)
                if prep is not None and part == 0:
                    e.wait_ge(S["xlo_done"], 8 * prep + c + 1)
                wt = WS[:, slot, 1 if part == 2 else 0, 128 * c:128 * c + 128]
                xt = (HL if part == 1 else HH)[:, c, 512 * h:512 * h + 512]
                last = e.matmul(ps, wt, xt, start=g == 0, stop=g == 23)
            if b == 24:
                last.then_inc(S["fill_done"], 1)

        def tv(P, par, vv, kind):
            e.wait_ge(S["fill_evac"], 6 * P + vv + 1)
            for k in range(4):
                c = 512 * vv + 128 * k
                last = e.transpose(PS[:, PV_BANK, 128 * k:128 * k + 128], QR[:, par, c:c + 128], IDENT[:, :])
            last.then_inc(S["tv_done"], 1)

        def qk(P, par, n, kind, fresh=False):
            k0, nk = key_tiles(kind, n)
            e.wait_ge(S["xy_dve"], 8 * P + n + 1)
            for m in range(2):
                e.wait_ge(S["ttr_done"], 1 + 16 * P + (0 if fresh else 2 * n + m - 1))
                for c in range(0, nk, 4):
                    wd = 128 * min(4, nk - c)
                    k = 128 * (k0 + c)
                    ps = PS[:, S_BANK[m] + c // 4, 0:wd]
                    e.matmul(ps, XY[:, m, :], KS[:, par, m, k:k + wd], start=True, stop=False)
                    last = e.matmul(ps, XY[:, 2 + m, :], KS[:, par, m, k:k + wd], start=False, stop=True)
                last.then_inc(S["qk_done"], 1)

        def turn(P, n, m, kind):
            k0, nk = key_tiles(kind, n)
            e.wait_ge(S["p0_ready" if m == 0 else "p1_ready"], 8 * P + n + 1)
            e.wait_ge(S["lo_done"], 1 + t_count(P, n, m, kind) - 1)
            src = e_tile(kind, n, m)
            for k in range(nk):
                last = e.transpose(PS[:, T_BANK + k // 4, 128 * (k % 4):128 * (k % 4) + 128],
                                   src[:, 128 * k:128 * k + 128], IDENT[:, :])
            last.then_inc(S["t_done"], 1)

        def pv(P, par, n, m, kind):
            b = m if kind != "C" else (n // 2) % 2
            u = unit(P, n, m, kind)
            e.wait_ge(S["lo_done"], 1 + t_count(P, n, m, kind))
            e.wait_ge(S["y_done"], 1 + u)
            e.wait_ge(S["vlo_done"], 2 * P + 2)
            a0, na = key_tiles(kind, n - 1)
            b0, nb = key_tiles(kind, n)
            both = list(range(max(a0, b0), min(a0 + na, b0 + nb)))
            tiles = [(k, 0, 256) for k in both]
            tiles += [(k, 0, 128) for k in range(a0, a0 + na) if k not in both]
            tiles += [(k, 128, 256) for k in range(b0, b0 + nb) if k not in both]
            todo = []
            for k, lo_, hi_ in tiles:
                if kind == "C":
                    passes = [(0, 0), (0, 1), (128, 0)]
                    todo += [(VS[:, par, k, v:v + 128], AT[:, b, k, p, lo_:hi_], lo_, hi_) for v, p in passes]
                else:
                    v = VS[:, par, k, 128 * m:128 * m + 128]
                    todo += [(v, AT[:, b, k, p, lo_:hi_], lo_, hi_) for p in range(2)]
            for i, (v, p, lo_, hi_) in enumerate(todo):
                last = e.matmul(PS[:, PV_BANK, lo_:hi_], v, p, start=i == 0, stop=i == len(todo) - 1)
            last.then_inc(S["pv_done"], 1)

        def first_chunk(layer, c):
            for k in range(2):
                fill(8 * layer, 0, k, 3 * c, 3 * c + 3, layer, prep=2 * layer, bank=FIRST_BANKS[k])

        def attention(layer):
            P0, kind, N = 8 * layer, "AC"[layer], 2 * layer
            def first(k):
                fill(P0, 0, k, 0, 24, layer, bank=FIRST_BANKS[k])

            for c in range(EARLY if layer else 0, KC):
                first_chunk(layer, c)
            if layer:
                e.wait_ge(S["d_free"], 4 + 16 * FT)
            ssq(N)
            first(2)
            spread_rstd(N)
            tv(P0, 0, 0, kind)
            first(3)
            e.wait_ge(S["vlo_done"], 2 * P0 + 1)
            tv(P0, 0, 1, kind)
            first(4)
            e.wait_ge(S["fill_evac"], 6 * P0 + 1)
            first(5)

            def start(P, par, kind):
                qk(P, par, 0, kind, fresh=True)

            def body(P, par, kind, nxt, looks):
                for n in range(NQ):
                    part = FILLS[kind][n] if nxt else [None] * 3
                    if kind != "C":
                        turn(P, n, 0, kind)
                    if n < NQ - 1:
                        qk(P, par, n + 1, kind)
                    elif looks:
                        qk(P + 1, 1 - par, 0, kind)
                    if part[0]:
                        fill(P + 1, 1 - par, *part[0], layer)
                    turn(P, n, 1 if kind != "C" else 0, kind)
                    if part[1]:
                        fill(P + 1, 1 - par, *part[1], layer)
                    if nxt and n in TV_AT[kind]:
                        e.wait_ge(S["y_done"], 1 + unit(P, n, 0, kind))
                        tv(P + 1, 1 - par, TV_AT[kind][n], kind)
                    if n % 2 and kind != "C":
                        if nxt and n - 1 in TV_AT[kind]:
                            e.wait_ge(S["vlo_done"], 2 * (P + 1) + TV_AT[kind][n - 1] + 1)
                        pv(P, par, n, 0, kind)
                    if kind == "C" and n in (2, 4, 6):
                        if nxt and n - 1 in TV_AT[kind]:
                            e.wait_ge(S["vlo_done"], 2 * (P + 1) + TV_AT[kind][n - 1] + 1)
                        pv(P, par, n - 1, 0, kind)
                    if part[2]:
                        fill(P + 1, 1 - par, *part[2], layer)
                    if kind == "C" and nxt is None and n:
                        if n == 1:
                            e.wait_ge(S["fill_evac"], 96)
                        y_sums(n - 1)
                    if n % 2 and kind != "C":
                        pv(P, par, n, 1, kind)
                if kind == "C":
                    pv(P, par, NQ - 1, 0, kind)

            iterations(e, body, start, layer)

        def out_projection(o):
            if o == 1:
                e.wait_ge(S["yrec_done"], 1)
                for k in range(KC):
                    if k == KC - 1:
                        y_sums(k)
                        e.wait_ge(S["yrec_done"], 2)
                    if k >= 2:
                        e.wait_ge(S["ynorm_done"], k - 1)
                    spread(RT[:, k, :], 2 * (k % 2), "yspread_done")
                e.wait_ge(S["ynorm_done"], KC)
            with e.Fori(0, KC // 2) as i:
                for b in range(2):
                    j = 2 * i + b
                    w = W_OUT[o] + j
                    for h in range(2):
                        ps = PS[:, 2 * b + h, :]
                        e.wait_ge(S["op_free"], 16 * o + 2 * j + h + 1)
                        for k in range(KC):
                            if h == 0 and k % 4 == 0:
                                e.wait_ge(S["w_lo"], 2 * w + 1 + k // 4)
                            if h == 0 and b == 0:
                                e.wait_ge(S["ylo_done"], 8 * o + k + 1)
                            last = three(ps, WS[:, b, 0, 128 * k:128 * k + 128], WS[:, b, 1, 128 * k:128 * k + 128],
                                         HH[:, k, 512 * h:512 * h + 512], HL[:, k, 512 * h:512 * h + 512],
                                         k == 0, k == KC - 1)
                        last.then_inc(S["op_done"], 1)

        def ffn(n):
            N = 2 * n + 1

            def body(t, first=False, last=False):
                TT = FT * n + t
                w = W_FFN[n] + 2 * t
                if first:
                    e.wait_ge(S["op_free"], 4 + 16 * (n + 1))
                e_next = 0
                for step in range(16):
                    if not last:
                        gate, h, c0 = step < 8, (step // 4) % 2, 2 * (step % 4)
                        slot = 0 if gate else 1
                        ps = PS[:, (G_BANK if gate else U_BANK) + h, :]
                        if step == 0:
                            e.wait_ge(S["sil_done"], TT)
                        if step == 4 and first:
                            ssq(N)
                        if step == 8:
                            if first:
                                spread_rstd(N)
                            e.wait_ge(S["umul_done"], TT)
                        for c in (c0, c0 + 1):
                            if h == 0 and c % 4 == 0:
                                e.wait_ge(S["w_lo"], 2 * (w + slot) + 1 + c // 4)
                            if first and step < 4:
                                e.wait_ge(S["xlo_done"], 8 * N + c + 1)
                            mm = three(ps, WS[:, slot, 0, 128 * c:128 * c + 128], WS[:, slot, 1, 128 * c:128 * c + 128],
                                       FH[:, c, 512 * h:512 * h + 512], FL[:, c, 512 * h:512 * h + 512],
                                       c == 0, c == KC - 1)
                        if step in (7, 15):
                            mm.then_inc(S["g_done" if gate else "u_done"], 1)
                    if not first and step >= 4:
                        until = 16 if step == 15 else (step - 3) * 16 // 12
                        while e_next < until:
                            ev = e_next
                            if ev == 0:
                                e.wait_ge(S["alo_done"], TT)
                                e.wait_ge(S["d_lo"], 1 + TT)
                                e.wait_ge(S["rstd_done"], N + 1)
                            e.wait_ge(S["d_free"], 16 * (TT - 1) + ev + 1)
                            j, h = ev // 2, ev % 2
                            mm = three(PS[:, D_BANK + ev % 4, :], DS[:, 0, 128 * j:128 * j + 128],
                                       DS[:, 1, 128 * j:128 * j + 128], AH[:, 512 * h:512 * h + 512],
                                       AL[:, 512 * h:512 * h + 512], True, True)
                            mm.then_inc(S["d_done"], 1)
                            e_next += 1
                            if last and n == 0 and ev % 2 and ev // 2 >= KC - EARLY:
                                first_chunk(1, ev // 2 - (KC - EARLY))

            body(0, first=True)
            with e.Fori(1, FT) as t:
                body(t)
            body(FT, last=True)

        e.wait_ge(S["ident_ready"], 2)
        e.sem_inc(S["pv_done"], 2)
        for name in ("qk_done", "op_done", "d_done"):
            e.sem_inc(S[name], 1)
        attention(0)
        out_projection(0)
        ffn(0)
        attention(1)
        out_projection(1)
        ffn(1)
        ssq(4)
        spread_rstd(4)

    with nc.Block() as block:
        @block.sync
        def _(e):
            sync_program(e)

        @block.gpsimd
        def _(e):
            pool_program(e)

        @block.scalar
        def _(e):
            act_program(e)

        @block.vector
        def _(e):
            dve_program(e)

        @block.tensor
        def _(e):
            pe_program(e)


def tables():
    p = np.arange(128)[:, None]
    d = np.abs(np.arange(BIAS_W)[None, :] - 128 * (NQ - 1) - p)
    slopes = np.exp2(-np.arange(1, 9, dtype=np.float64))
    count = sum(((d % dil == 0) & (d <= win // 2)).astype(int) for win, dil in ((128, 1), (512, 4), (2048, 16)))
    fixed = np.where(count > 0, -np.log(np.maximum(count, 1)), BIG)
    a = slopes[:, None, None] * d[None] + fixed[None]
    a = a.reshape(4, 2, 128, BIAS_W).transpose(0, 2, 1, 3)
    c = slopes[:, None, None] * d[None]
    return a.astype(np.float32), c.astype(np.float32)


def table_b_index():
    par, col = np.divmod(np.arange(128), GRID)
    first = np.clip(col - COLS // 2, 0, GRID - COLS)
    k = np.arange(GRID)
    inside = (k >= first[:, None]) & (k < first[:, None] + COLS)
    dc = k[None] - col[:, None] + COLS - 1
    rows = []
    for start, n, window in ((-6, EDGE_ROWS, None), (-4, MID_ROWS, (-4, 3))):
        for u in range(start, start + n):
            dr = u - par + ROWS - 1
            ok = (dr >= 0) & (dr < 2 * ROWS - 1)
            if window:
                ok &= (u - par >= window[0]) & (u - par <= window[1])
            rows.append(np.where(ok[:, None] & inside, dr[:, None] * (2 * COLS - 1) + dc, -1))
    return np.concatenate(rows, axis=1)


def strips(w, order):
    w = w.reshape(KC, 128, -1)
    s = np.stack([w[:, :, c:c + 128] for c in order])
    s = s.reshape(len(order), 2, 4, 128, 128).transpose(0, 1, 3, 2, 4)
    return s.reshape(len(order), 2, 128, 512)


def kernel(x, a0_norm, a0_w_in, a0_w_out, a0_rpb, f0_norm, f0_w_gate, f0_w_up, f0_w_down,
           a1_norm, a1_w_qkv, a1_w_out, a1_lam_q1, a1_lam_k1, a1_lam_q2, a1_lam_k2, a1_subln,
           f1_norm, f1_w_gate, f1_w_up, f1_w_down, final_norm):
    import concourse.bacc as bacc
    from concourse.bass_utils import run_bass_kernel_spmd

    n = lambda a: np.asarray(a)
    order0 = [base + 128 * p + off for base in (0, 1536) for p in range(4) for off in (1024, 512, 0)]
    order1 = [128 * h + off for h in range(8) for off in (2048, 1024, 0)]

    def gate_up(g, u):
        s = np.stack([strips(n(g), range(0, F, 128)), strips(n(u), range(0, F, 128))], axis=1)
        return s.reshape(2 * FT, 2, 128, 512)

    cols = list(range(0, D, 128))
    wstrips = np.concatenate([
        strips(n(a0_w_in), order0), strips(n(a0_w_out), cols), gate_up(f0_w_gate, f0_w_up),
        strips(n(a1_w_qkv), order1), strips(n(a1_w_out), cols), gate_up(f1_w_gate, f1_w_up)])
    wdown = np.concatenate([n(f0_w_down), n(f1_w_down)]).reshape(2 * FT, 128, D)
    gains = np.stack([n(g).reshape(KC, 128).T for g in (a0_norm, f0_norm, a1_norm, f1_norm, final_norm)], axis=1)
    lams = np.stack([n(a1_lam_q1), n(a1_lam_k1), n(a1_lam_q2), n(a1_lam_k2)])
    ali_a, ali_c = tables()
    index = table_b_index()
    rpb = n(a0_rpb).reshape(8, -1)
    tab_b = np.where(index < 0, np.float32(-BIG), rpb[:, np.maximum(index, 0)]).astype(np.float32)
    tab_b = tab_b.reshape(4, 2, 128, TAB_B).transpose(0, 2, 1, 3)
    list_a = np.zeros((5, 128, 2, BIAS_W), np.float32)
    list_a[:4] = ali_a
    list_a[4, :, :, :TAB_B] = tab_b[0]

    arrays = {
        "x": n(x).reshape(T, KC, 128).transpose(2, 1, 0), "wstrips": wstrips, "wdown": wdown, "gains": gains,
        "subln": n(a1_subln).reshape(128, 1), "lams": lams, "ali_a": list_a, "ali_c": ali_c, "tab_b": tab_b,
    }
    arrays = {k: np.ascontiguousarray(v) for k, v in arrays.items()}
    nc = bacc.Bacc("TRN2", target_bir_lowering=False, num_devices=1)
    aps = [nc.dram_tensor(k, list(v.shape), mybir.dt.from_np(v.dtype), kind="ExternalInput").ap()
           for k, v in arrays.items()]
    out = nc.dram_tensor("out", [128, KC, T], mybir.dt.float32, kind="ExternalOutput").ap()
    build(nc, *aps, out)
    r = run_bass_kernel_spmd(nc, [arrays], core_ids=[0])
    y = np.asarray(r.results[0]["out"])
    return y.transpose(2, 1, 0).reshape(1, T, D)
```
